# Optimizing a Trainium2 kernel written in Bass

```python
import numpy as np
import jax
import jax.numpy as jnp
from jax import lax

D_MODEL = 1024
BATCH = 1
SEQ = 512
DEPTH = 1

RET_HEADS = 4
RET_QK_DIM = 128
RET_V_DIM = 256
MLSTM_HEADS = 4
MLSTM_QK_DIM = 128
MLSTM_V_DIM = 256
CONV_WIDTH = 4
CHUNK = 128
ROPE_BASE = 10000.0
N_GROUPS = 4
EXPERTS_PER_GROUP = 8
N_EXPERTS = N_GROUPS * EXPERTS_PER_GROUP
TOP_K = 2
D_EXPERT = 512
MOE_BLOCK = 128
NORM_EPS = 1e-6

RET_QK = RET_HEADS * RET_QK_DIM
RET_V = RET_HEADS * RET_V_DIM
M_QK = MLSTM_HEADS * MLSTM_QK_DIM
M_V = MLSTM_HEADS * MLSTM_V_DIM
IN_SPLITS = (RET_QK, RET_QK, RET_V, RET_V, M_QK, M_QK, M_V, M_V, MLSTM_HEADS, MLSTM_HEADS, D_MODEL, D_MODEL)
D_IN = RET_QK * 2 + RET_V * 2 + M_QK * 2 + M_V * 2 + MLSTM_HEADS * 2 + D_MODEL * 2

kernel_name = "hybrid_retention_mlstm_hmoe"

def split_points(widths):
    pts, acc = [], 0
    for w in widths[:-1]:
        acc += w
        pts.append(acc)
    return pts

def rms_norm(x, w):
    xf = x.astype(jnp.float32)
    y = xf * lax.rsqrt(jnp.mean(xf * xf, axis=-1, keepdims=True) + NORM_EPS)
    return (y * w.astype(jnp.float32)).astype(x.dtype)

def head_rms_norm(xh):
    B, S, H, d = xh.shape
    y = xh * lax.rsqrt(jnp.mean(xh * xh, axis=-1, keepdims=True) + NORM_EPS)
    return y.reshape(B, S, H * d)

def rotary(x, positions):
    d = x.shape[-1]
    inv_freq = 1.0 / (ROPE_BASE ** (jnp.arange(0, d, 2, dtype=jnp.float32) / d))
    ang = positions.astype(jnp.float32)[:, None] * inv_freq[None, :]
    cos = jnp.cos(ang)[None, :, None, :]
    sin = jnp.sin(ang)[None, :, None, :]
    x1, x2 = jnp.split(x, 2, axis=-1)
    return jnp.concatenate([x1 * cos - x2 * sin, x2 * cos + x1 * sin], axis=-1)

def to_chunks(t):
    B, S, H, d = t.shape
    return t.reshape(B, S // CHUNK, CHUNK, H, d).transpose(1, 0, 3, 2, 4)

def from_chunks(t):
    nc, B, H, L, d = t.shape
    return t.transpose(1, 0, 3, 2, 4).reshape(B, nc * L, H, d)

def retention_chunkwise(q, k, v, log_gamma):
    B, S, H, dk = q.shape
    dv = v.shape[-1]
    idx = jnp.arange(CHUNK, dtype=jnp.float32)
    rel = idx[:, None] - idx[None, :]
    causal = rel >= 0
    decay_mask = jnp.where(causal[None], jnp.exp(log_gamma[:, None, None] * jnp.where(causal, rel, 0.0)[None]), 0.0)
    q_decay = jnp.exp(log_gamma[:, None] * (idx + 1.0)[None, :])
    k_decay = jnp.exp(log_gamma[:, None] * (CHUNK - 1.0 - idx)[None, :])
    chunk_decay = jnp.exp(log_gamma * CHUNK)

    def step(R, inp):
        qi, ki, vi = inp
        s = jnp.einsum('bhld,bhmd->bhlm', qi, ki) * decay_mask[None]
        o = (jnp.einsum('bhlm,bhme->bhle', s, vi)
             + jnp.einsum('bhld,bhde->bhle', qi, R) * q_decay[None, :, :, None])
        R = (R * chunk_decay[None, :, None, None]
             + jnp.einsum('bhld,bhle->bhde', ki * k_decay[None, :, :, None], vi))
        return R, o

    R0 = jnp.zeros((B, H, dk, dv), jnp.float32)
    _, o = lax.scan(step, R0, (to_chunks(q), to_chunks(k), to_chunks(v)))
    return from_chunks(o)

def mlstm_chunkwise(q, k, v, i_pre, f_pre):
    B, S, H, dk = q.shape
    dv = v.shape[-1]
    nc = S // CHUNK
    log_f = jax.nn.log_sigmoid(f_pre)
    gate_chunks = lambda g: g.reshape(B, nc, CHUNK, H).transpose(1, 0, 3, 2)
    causal = jnp.tril(jnp.ones((CHUNK, CHUNK), dtype=bool))

    def step(carry, inp):
        C, n, m = carry
        qi, ki, vi, ii, lfi = inp
        b = jnp.cumsum(lfi, axis=-1)
        a = b + m[..., None]
        dmat = jnp.where(causal, b[..., :, None] - b[..., None, :] + ii[..., None, :], -jnp.inf)
        m_t = jnp.maximum(a, jnp.max(dmat, axis=-1))
        w_inter = jnp.exp(a - m_t)
        s = jnp.einsum('bhld,bhmd->bhlm', qi, ki) * jnp.exp(dmat - m_t[..., None])
        num = jnp.einsum('bhlm,bhme->bhle', s, vi) + jnp.einsum('bhld,bhde->bhle', qi, C) * w_inter[..., None]
        den = jnp.sum(s, axis=-1) + jnp.einsum('bhld,bhd->bhl', qi, n) * w_inter
        h = num / jnp.maximum(jnp.abs(den), jnp.exp(-m_t))[..., None]
        b_last = b[..., -1]
        g = b_last[..., None] - b + ii
        m_new = jnp.maximum(b_last + m, jnp.max(g, axis=-1))
        keep = jnp.exp(b_last + m - m_new)
        wk = ki * jnp.exp(g - m_new[..., None])[..., None]
        C = C * keep[..., None, None] + jnp.einsum('bhld,bhle->bhde', wk, vi)
        n = n * keep[..., None] + jnp.sum(wk, axis=-2)
        return (C, n, m_new), h

    carry0 = (jnp.zeros((B, H, dk, dv), jnp.float32), jnp.zeros((B, H, dk), jnp.float32),
              jnp.zeros((B, H), jnp.float32))
    _, h = lax.scan(step, carry0, (to_chunks(q), to_chunks(k), to_chunks(v), gate_chunks(i_pre), gate_chunks(log_f)))
    return from_chunks(h)

def causal_depthwise_conv(u, w, b):
    y = lax.conv_general_dilated(u, w.astype(u.dtype), window_strides=(1,), padding=[(w.shape[0] - 1, 0)],
                                 dimension_numbers=('NWC', 'WIO', 'NWC'), feature_group_count=u.shape[-1])
    return y + b.astype(u.dtype)

def hybrid_mixer(h, positions, w_in, ret_gn_w, w_ret_branch, conv_w, conv_b, b_i, b_f, mlstm_gn_w,
                 w_mlstm_branch, w_out):
    B, S, _ = h.shape
    f32 = jnp.float32
    proj = h @ w_in
    (r_q, r_k, r_v, r_g, m_q, m_k, m_v, m_o, m_i, m_f, gate_r, gate_m) = jnp.split(proj, split_points(IN_SPLITS), axis=-1)

    log_gamma = jnp.log(1.0 - 2.0 ** (-5.0 - jnp.arange(RET_HEADS, dtype=f32)))
    rq = rotary(r_q.reshape(B, S, RET_HEADS, RET_QK_DIM).astype(f32), positions)
    rk = rotary(r_k.reshape(B, S, RET_HEADS, RET_QK_DIM).astype(f32), positions) * (RET_QK_DIM ** -0.5)
    rv = r_v.reshape(B, S, RET_HEADS, RET_V_DIM).astype(f32)
    ret = head_rms_norm(retention_chunkwise(rq, rk, rv, log_gamma))
    ret = ret * ret_gn_w.astype(f32) * jax.nn.silu(r_g.astype(f32))
    y_ret = ret.astype(h.dtype) @ w_ret_branch

    qk = jax.nn.silu(causal_depthwise_conv(jnp.concatenate([m_q, m_k], axis=-1), conv_w, conv_b))
    mq, mk = jnp.split(qk, 2, axis=-1)
    mq = mq.reshape(B, S, MLSTM_HEADS, MLSTM_QK_DIM).astype(f32)
    mk = mk.reshape(B, S, MLSTM_HEADS, MLSTM_QK_DIM).astype(f32) * (MLSTM_QK_DIM ** -0.5)
    mv = m_v.reshape(B, S, MLSTM_HEADS, MLSTM_V_DIM).astype(f32)
    i_pre = m_i.astype(f32) + b_i.astype(f32)
    f_pre = m_f.astype(f32) + b_f.astype(f32)
    hm = mlstm_chunkwise(mq, mk, mv, i_pre, f_pre).reshape(B, S, M_V) * jax.nn.sigmoid(m_o.astype(f32))
    hm = head_rms_norm(hm.reshape(B, S, MLSTM_HEADS, MLSTM_V_DIM)) * mlstm_gn_w.astype(f32)
    y_m = hm.astype(h.dtype) @ w_mlstm_branch

    merged = jax.nn.sigmoid(gate_r) * y_ret + jax.nn.sigmoid(gate_m) * y_m
    return merged @ w_out

def hierarchical_moe(h, w_group, b_group, w_expert_router, b_expert_router, w_gate, w_up, w_down):
    B, S, D = h.shape
    T = B * S
    xt = h.reshape(T, D)
    xf = xt.astype(jnp.float32)
    group_prob = jax.nn.softmax(xf @ w_group.astype(jnp.float32) + b_group.astype(jnp.float32), axis=-1)
    g_w, g_idx = lax.top_k(group_prob, 1)
    e_logits = (xf @ w_expert_router.astype(jnp.float32) + b_expert_router.astype(jnp.float32)).reshape(T, N_GROUPS, EXPERTS_PER_GROUP)
    sel_logits = e_logits[jnp.arange(T), g_idx[:, 0]]
    top_logits, e_idx = lax.top_k(sel_logits, TOP_K)
    e_w = jax.nn.softmax(top_logits, axis=-1)
    weights = g_w * e_w
    expert_id = g_idx * EXPERTS_PER_GROUP + e_idx

    A = T * TOP_K
    P = A + N_EXPERTS * MOE_BLOCK
    n_blocks = P // MOE_BLOCK
    flat_e = expert_id.reshape(A).astype(jnp.int32)
    flat_tok = jnp.repeat(jnp.arange(T, dtype=jnp.int32), TOP_K)
    flat_w = weights.reshape(A)
    order = jnp.argsort(flat_e)
    se = flat_e[order]
    counts = jnp.bincount(flat_e, length=N_EXPERTS)
    padded = ((counts + MOE_BLOCK - 1) // MOE_BLOCK) * MOE_BLOCK
    start = jnp.cumsum(counts) - counts
    pend = jnp.cumsum(padded)
    pstart = pend - padded
    dest = pstart[se] + (jnp.arange(A, dtype=jnp.int32) - start[se])
    slot_tok = jnp.full((P,), T, dtype=jnp.int32).at[dest].set(flat_tok[order])
    slot_w = jnp.zeros((P,), jnp.float32).at[dest].set(flat_w[order])
    blk_start = jnp.arange(n_blocks, dtype=jnp.int32) * MOE_BLOCK
    blk_e = jnp.minimum(jnp.sum(blk_start[:, None] >= pend[None, :], axis=-1), N_EXPERTS - 1)
    x_pad = jnp.concatenate([xt, jnp.zeros((1, D), xt.dtype)], axis=0)
    xs = x_pad[slot_tok].reshape(n_blocks, MOE_BLOCK, D)

    def expert_block(args):
        xb, e = args
        return (jax.nn.silu(xb @ w_gate[e]) * (xb @ w_up[e])) @ w_down[e]

    ys = lax.map(expert_block, (xs, blk_e)).reshape(P, D)
    ys = ys * slot_w[:, None].astype(ys.dtype)
    out = jax.ops.segment_sum(ys, slot_tok, num_segments=T + 1)[:T]
    return out.reshape(B, S, D)

def setup_inputs(seed: int = 0) -> dict:
    key = jax.random.key(seed)
    ks = jax.random.split(key, 24)
    L, D = DEPTH, D_MODEL

    def nrm(k, shape, scale):
        return jax.random.normal(k, shape, jnp.float32) * scale

    return {
        "x": nrm(ks[0], (BATCH, SEQ, D), 1.0),
        "norm_mix_w": 1.0 + nrm(ks[1], (L, D), 0.02),
        "w_in": nrm(ks[2], (L, D, D_IN), D ** -0.5),
        "ret_gn_w": 1.0 + nrm(ks[3], (L, RET_V), 0.02),
        "w_ret_branch": nrm(ks[4], (L, RET_V, D), RET_V ** -0.5),
        "mlstm_conv_w": nrm(ks[5], (L, CONV_WIDTH, 1, 2 * M_QK), CONV_WIDTH ** -0.5),
        "mlstm_conv_b": nrm(ks[6], (L, 2 * M_QK), 0.01),
        "b_igate": nrm(ks[7], (L, MLSTM_HEADS), 0.1),
        "b_fgate": jnp.linspace(3.0, 6.0, MLSTM_HEADS, dtype=jnp.float32)[None, :] + nrm(ks[8], (L, MLSTM_HEADS), 0.1),
        "mlstm_gn_w": 1.0 + nrm(ks[9], (L, M_V), 0.02),
        "w_mlstm_branch": nrm(ks[10], (L, M_V, D), M_V ** -0.5),
        "w_out": nrm(ks[11], (L, D, D), D ** -0.5),
        "norm_ffn_w": 1.0 + nrm(ks[12], (L, D), 0.02),
        "w_group": nrm(ks[13], (L, D, N_GROUPS), D ** -0.5),
        "b_group": nrm(ks[14], (L, N_GROUPS), 0.01),
        "w_expert_router": nrm(ks[15], (L, D, N_EXPERTS), D ** -0.5),
        "b_expert_router": nrm(ks[16], (L, N_EXPERTS), 0.01),
        "w_gate": nrm(ks[17], (L, N_EXPERTS, D, D_EXPERT), D ** -0.5),
        "w_up": nrm(ks[18], (L, N_EXPERTS, D, D_EXPERT), D ** -0.5),
        "w_down": nrm(ks[19], (L, N_EXPERTS, D_EXPERT, D), D_EXPERT ** -0.5),
        "norm_final_w": 1.0 + nrm(ks[20], (D,), 0.02),
    }

def reference(x, norm_mix_w, w_in, ret_gn_w, w_ret_branch, mlstm_conv_w, mlstm_conv_b, b_igate, b_fgate,
              mlstm_gn_w, w_mlstm_branch, w_out, norm_ffn_w, w_group, b_group, w_expert_router,
              b_expert_router, w_gate, w_up, w_down, norm_final_w):
    positions = jnp.arange(x.shape[1], dtype=jnp.int32)
    for layer in range(DEPTH):
        h = rms_norm(x, norm_mix_w[layer])
        x = x + hybrid_mixer(h, positions, w_in[layer], ret_gn_w[layer], w_ret_branch[layer], mlstm_conv_w[layer],
                             mlstm_conv_b[layer], b_igate[layer], b_fgate[layer], mlstm_gn_w[layer],
                             w_mlstm_branch[layer], w_out[layer])
        h = rms_norm(x, norm_ffn_w[layer])
        x = x + hierarchical_moe(h, w_group[layer], b_group[layer], w_expert_router[layer], b_expert_router[layer],
                                 w_gate[layer], w_up[layer], w_down[layer])
    return rms_norm(x, norm_final_w)


_drawn_inputs = setup_inputs


def setup_inputs(seed=0):
    import zlib

    import numpy as np

    out = dict(_drawn_inputs(seed))
    spreads = {}
    factors = {'ret_gn_w': 16.858,
     'mlstm_conv_b': 4.263,
     'b_igate': 64.0,
     'mlstm_gn_w': 10.724,
     'b_group': 16.979,
     'b_expert_router': 14.912,
     'norm_final_w': 8.726,
     'norm_ffn_w': 5.019}
    for name, (base, spread) in spreads.items():
        noise = np.random.default_rng([zlib.crc32(name.encode()), seed]).standard_normal(out[name].shape)
        drawn = base * np.exp(spread * noise) if base else spread * noise
        out[name] = jnp.asarray(drawn.astype(out[name].dtype))
    for name, factor in factors.items():
        out[name] = (out[name] * factor).astype(out[name].dtype)
    return out
```

```python
import concourse.bass as bass
from concourse import mybir
from contextlib import ExitStack

F32 = mybir.dt.float32
F32R = mybir.dt.float32r
F16 = mybir.dt.float16
I32 = mybir.dt.int32
ALU = mybir.AluOpType
ACT = mybir.ActivationFunctionType
AX = mybir.AxisListType

P = 128
T = 512
D = 1024
TT = T // P
KD = D // P
H = 4
DK = 128
DV = 256
DA = DV + 1
NE, NG, EG = 32, 4, 8
FE = 512
KF = FE // P
CAP = 64
ROUNDS = T // CAP
EPS = 1e-6
BIG = 1e30
COUNT_SHIFT = 1000
KB = 1024

C_RQ, C_RK, C_RV, C_RG = 0, 512, 1024, 2048
C_MQ, C_MK, C_MV, C_MO = 3072, 3584, 4096, 5120
C_IF, C_GR, C_GM = 6144, 6152, 7176
B_RQ, B_RK, B_RV, B_MQ, B_MK, B_MV, B_RG, B_GR, B_GM, B_MO, B_WR, B_WM, B_WO = 0, 1, 2, 4, 5, 6, 8, 10, 12, 14, 16, 18, 20
BLOCKS = 22
IN_COLS = [C_RQ, C_RK, C_RV, C_RV + 512, C_MQ, C_MK, C_MV, C_MV + 512, C_RG, C_RG + 512,
           C_GR, C_GR + 512, C_GM, C_GM + 512, C_MO, C_MO + 512]
CHANNEL_MAJOR = {B_MQ, B_MK, B_GR, B_GR + 1, B_GM, B_GM + 1, B_WR, B_WR + 1, B_WM, B_WM + 1}
MIX_PAIRS = 4 * BLOCKS
RING = 4
LEAD = RING - 1
MIX_RAW = 3
MOE_RAW = 12
E_PAIRS = 12
R_PAIRS = NE * E_PAIRS

K_IDENT = 0
K_RMASK = K_IDENT + P
K_NOTYET = K_RMASK + H * P
K_BEFORE = K_NOTYET + P
K_QDEC = K_BEFORE + P
K_SEL64 = K_QDEC + H * P
K_COS = K_SEL64 + CAP
K_SIN = K_COS + TT * 64
K_KDEC = K_SIN + TT * 64
K_SLOT = K_KDEC + H
K_PRIO = K_SLOT + CAP
K_TOK = K_PRIO + NE
K_SELH = K_TOK + 2 * TT
K_END = K_SELH + H * P

GAMMA = [1.0 - 2.0 ** (-5.0 - h) for h in range(H)]


def hybrid_block(nc, x, norm_mix_w, w_in, ret_gn_w, w_ret, conv_w, conv_b, b_i, b_f, mlstm_gn_w, w_mlstm, w_out,
                 norm_ffn_w, w_group, b_group, w_router, b_router, w_gate, w_up, w_down, norm_final_w, consts, out):
    ctx = ExitStack()
    with ctx:
        base = -(-nc.sbuf_base // 64) * 64

        def at(name, kib, shape, dt=F32):
            return nc.alloc_sbuf_tensor_at(name, shape, dt, offset=base + int(kib * KB))

        def sem(name):
            return ctx.enter_context(nc.semaphore(name))

        hTh = at("hTh", 0, [P, KD, T], F32R)
        hTl = at("hTl", 16, [P, KD, T], F32R)
        mixTh = at("mixTh", 0, [P, KD, T], F32R)
        mixTl = at("mixTl", 16, [P, KD, T], F32R)
        rqn = at("rqn", 32, [P, TT, 512])
        rqT = at("rqT", 40, [P, H, T])
        rkT = at("rkT", 48, [P, H, T])
        rkn = at("rkn", 56, [P, TT, 512])
        dT = at("dT", 32, [P, H, T])
        Cst = at("Cst", 40, [P, H, DA])
        retTh = at("retTh", 32, [P, KD, T], F32R)
        retTl = at("retTl", 48, [P, KD, T], F32R)
        mrgTh = at("mrgTh", 32, [P, KD, T], F32R)
        mrgTl = at("mrgTl", 48, [P, KD, T], F32R)
        rvo = at("rvo", 64, [P, TT, D])
        msg = at("msg", 64, [P, 2, 512])
        convx = at("convx", 80, [P, 4, 3 + T])
        rtmp = at("rtmp", 88.25, [P, 2, 512])
        Rst = at("Rst", 88.25, [P, H, DV])
        csg = at("csg", 92.25, [P, T])
        selh = at("selh", 92.25, [H, H * P])
        rsg = at("rsg", 80, [P, 2, 512])
        mrg = at("mrg", 80, [P, KD, T])
        raw_moe = [at(f"raw_moe{s}", k, [P, 4, 512]) for s, k in
                   enumerate([64, 72, 0, 8, 16, 24, 80, 88, 32, 40, 48, 56])]
        wh = at("wh", 96, [P, RING, 2, 512], F32R)
        wl = at("wl", 112, [P, RING, 2, 512], F32R)
        xt = at("xt", 128, [P, TT, D])
        mva = at("mva", 128, [P, TT, H, DA])
        x2 = at("x2", 128, [P, TT, D])
        raw_mix = [at(f"raw_mix{s}", 144.5 + 8 * s, [P, 4, 512]) for s in range(MIX_RAW)]
        h2T = at("h2T", 144.5, [P, KD, T])
        hot = at("hot", 144.5, [P, TT, NE, CAP], F16)
        yo = at("yo", 144.5, [CAP, 2, D])
        yb = at("yb", 152.5, [CAP, D])
        gs = at("gs", 156.5, [P, 2, KF, P])
        yin = [at(f"yin{i}", 16 * i, [P, TT, D]) for i in range(2)]
        xg = at("xg", 160.5, [CAP, 2, D])
        xs0 = at("xs0", 168.5, [P, TT, D])
        wgh = at("wgh", 168.5, [P, KD, P], F32R)
        wgl = at("wgl", 172.5, [P, KD, P], F32R)
        grow = at("grow", 174.5, [H, 5, T])
        gbc = at("gbc", 184.5, [P, H, T])
        mqT = at("mqT", 168.5, [P, H, T])
        mkT = at("mkT", 176.5, [P, H, T])
        sgm = at("sgm", 168.5, [P, KD, T])
        h2 = at("h2", 168.5, [P, TT, D])
        xsp = [at(f"xsp{i}", 168.5 + 4 * i, [P, KD, P], F32R) for i in range(2)]
        hsp = at("hsp", 176.5, [P, KF, P], F32R)
        us = at("us", 178.5, [P, KF, P])
        sg = at("sg", 180.5, [P, KF * CAP])
        hf = at("hf", 181.5, [P, KF * CAP])
        wrow = at("wrow", 184.5, [P, D])
        wrt = at("wrt", 188.5, [P, KD, 36])
        brt = at("brt", 189.75, [P, 36])
        rt = at("rt", 190, [P, 8, TT * NE])
        kc = at("kc", 194, [P, K_SELH])
        rest = 194 + (K_SELH * 4 + 63) // 64 * 64 / KB

        class Small:
            top = rest

        def small(name, shape, dt=F32):
            n = 1
            for s in shape[1:]:
                n *= s
            t = at(name, Small.top, shape, dt)
            Small.top += -(-n * 4 // 32) * 32 / KB
            return t

        vrow = at("vrow", 188.5, [64, P])
        wgr = at("wgr", 189, [P, KD, 2 * H])
        vcol = small("vcol", [P, 64])
        bif = small("bif", [H, 2])
        stat = small("stat", [P, 4, 16])
        rret = small("rret", [P, 16])
        ssq = small("ssq", [P, 16])
        mprev = small("mprev", [H, TT + 1])
        gcol = small("gcol", [P, 5, 16])
        gex = small("gex", [P, 3, 16])
        rden = small("rden", [P, 2])
        st = small("st", [P, 2, P])
        over = Small.top - 2 * P * 4 / KB
        wk = small("wk", [P, 2, P])
        pv = at("pv", over, [P, TT, NE])
        val = at("val", over + 0.5, [P, TT, NE, 2], F16)
        lg = at("lg", over + 1, [P, TT, 36])
        iot = at("iot", over + 1.625, [P, CAP])
        slotw = small("slotw", [P, 2, TT])
        cnt = small("cnt", [1, 1], I32)
        tok_tab = small("tok_tab", [CAP, NE], I32)
        dst_tab = small("dst_tab", [CAP, NE], I32)
        tok_now = small("tok_now", [CAP, 2], I32)
        dst_now = small("dst_now", [CAP, 2], I32)
        onesq = small("onesq", [P, P])
        rsq = small("rsq", [P, DV])
        assert base + Small.top * KB <= nc.sbuf_usable_end, (base + Small.top * KB, nc.sbuf_usable_end)

        pj = ctx.enter_context(nc.psum_tensor("pj", [P, 4, 512], F32))
        cb = ctx.enter_context(nc.psum_tensor("cb", [P, 4, 512], F32))

        h_dram = nc.dram_tensor("h_scratch", [T, D], F32).ap()
        y_dram = nc.dram_tensor("y_scratch", [2 * T, D], F32).ap()

        c_in, x_in, v_in, wg_in, br_in, wr_in, xr_in = (sem(n) for n in (
            "consts_in", "x_in", "vectors_in", "gate_w_in", "router_in", "norm_row_in", "x_again_in"))
        raw_in = [sem(f"raw_in{s}") for s in range(MIX_RAW)]
        moe_in = [sem(f"moe_in{s}") for s in range(MOE_RAW)]
        wh_ok, wl_ok = sem("heads_ready"), sem("tails_ready")
        pair_used = sem("pairs_used")
        full = [sem(f"bank_full{i}") for i in range(4)]
        free = [sem(f"bank_free{i}") for i in range(4)]
        v_own, a_own = sem("vector_own"), sem("scalar_own")
        sq_ok, var_ok, root_ok = sem("squares"), sem("variance"), sem("root")
        vT, vC, xs_ok, zero_ok = sem("vectors_turned"), sem("vector_columns"), sem("x_scaled"), sem("memsets")
        it_ok = sem("slot_numbers_ready")
        hT_ps, hTh_ok, hTl_ok = sem("h_turned"), sem("h_heads"), sem("h_tails")
        gwh_ok, gwl_ok, g_ps, grow_a = sem("gate_w_heads"), sem("gate_w_tails"), sem("gates_in_psum"), sem("gate_rows_copied")
        f_abs, f_log, grow_ok, gtiny, gcol_ok = (sem(n) for n in (
            "forget_abs", "forget_log", "gate_rows_ready", "gate_columns_in_psum", "gate_columns_ready"))
        gex_in, gex_ok = sem("gate_exponents"), sem("gate_exps")
        gb_ps, gb_ok, dt_in, dt_ok, wint_ok = (sem(n) for n in (
            "G_broadcast", "G_copied", "decay_exponents", "decay_ready", "inter_weight_ready"))
        rope_ok, rqT_ps, rqT_ok, rkT_ps, rkT_ok = (sem(n) for n in (
            "rotated", "rq_turned", "rqT_ready", "rk_turned", "rkT_ready"))
        r_s, r_st, r_o, r_out, r_R = (sem(n) for n in ("ret_scores", "ret_masked", "ret_products", "ret_out", "ret_state"))
        conv_a, conv_v, conv_s, mqk_ok, wq_ok = (sem(n) for n in (
            "conv_first_tap", "conv_taps", "conv_sigmoid", "mqk_ready", "weighted_q_ready"))
        m_s, m_st, m_wk, m_o, m_rc, m_C, m_h = (sem(n) for n in (
            "ml_scores", "ml_weighted", "ml_keys", "ml_products", "ml_denominator", "ml_state", "ml_out"))
        rg_s, ret_ok, mo_v, hm_ok = sem("rgate_sigmoid"), sem("ret_gated"), sem("ml_gated"), sem("ml_normed")
        tr_ps, tr_h, tr_l = sem("out_turned"), sem("out_heads"), sem("out_tails")
        mg_ok, mgh_ok, mgl_ok = sem("merged"), sem("merged_heads"), sem("merged_tails")
        h2_ok, h2_out, h2T_ps, h2T_v, h2T_a = (sem(n) for n in (
            "h2_ready", "h2_in_dram", "h2_turned", "h2T_by_vector", "h2T_by_scalar"))
        lg_ps, e1_in, e1_ok, e2_in, e2_ok, hot_in, pos_ps, hot_ok, tab_ps, tab_ok, cnt_ok = (sem(n) for n in (
            "logits", "group_exponents", "group_exps", "expert_exponents", "expert_exps", "routed", "positions",
            "one_hot_ready", "table_in_psum", "table_ready", "counts_ready"))
        gat, sca, out_ok = [sem("gathered0"), sem("gathered1")], sem("scattered"), sem("outputs_out")
        tok_c, dst_c = sem("token_column"), sem("row_column")
        xT_ps, xh_ok, xl_ok = sem("expert_x_turned"), sem("expert_x_heads"), sem("expert_x_tails")
        g_f, u_f, gs_ok, us_ok, gt_ps, sg_ok, hq_ok, hf_ok, hh_ok, hl_ok, y_f, yb_ok, yo_ok = (sem(n) for n in (
            "gate_full", "up_full", "gate_copied", "up_copied", "gate_up_turned", "gate_sigmoid", "silu_ready", "hidden_ready",
            "hidden_heads", "hidden_tails", "y_full", "y_tails_copied", "y_ready"))
        y_in = [sem(f"y_in{t}") for t in range(TT)]
        scat_ok, x3_ok, fin_ok, out_in = sem("all_scattered"), sem("x3_ready"), sem("out_ready"), sem("out_stored")
        pe_past, pool_past = sem("tensor_past_waits"), sem("pool_past_waits")
        block = ctx.enter_context(nc.Block())

        def stage_of(st):
            if st < 2:
                return st, 0
            if st == R_PAIRS // 4 - 1:
                return 2, NE - 1
            kind = (st - 2) % 3
            return kind, 1 + (st - 2) // 3 - (kind == 2)

        def wait_pair_used(eng, r, i, t):
            used0 = 3 * BLOCKS + r * (3 * R_PAIRS // 4)
            if t < RING:
                if t < 3:
                    eng.wait_ge(pair_used, used0 - 3 + t + 1)
                elif isinstance(r, int):
                    eng.wait_ge(full[3], BLOCKS)
                else:
                    eng.wait_ge(y_f, r * NE)
                return
            st, j = divmod(t - RING, 4)
            if j < 3:
                eng.wait_ge(pair_used, used0 + 3 * st + j + 1 + i * 18)
            else:
                kind, e = stage_of(st)
                eng.wait_ge((g_f, u_f, y_f)[kind], r * NE + i * 2 + e + 1)

        def wait_mix_pair(eng, q):
            if q % 4 == 3:
                eng.wait_ge(full[3], q // 4 + 1)
            else:
                eng.wait_ge(pair_used, 3 * (q // 4) + q % 4 + 1)

        def moe_raw(t):
            m = t // 2
            return raw_moe[m % MOE_RAW][:, 2 * (t % 2):2 * (t % 2) + 2, :], m % MOE_RAW, m // MOE_RAW + 1

        LOADS = R_PAIRS // 2 // MOE_RAW

        @block.sync
        def _(sp):
            sp.dma_start(xt[:, :, :], x[0].rearrange("(t p) d -> p t d", p=P)).then_inc(x_in, 16)
            sp.dma_start(kc[:, :], consts[:, 0:K_SELH]).then_inc(c_in, 16)
            sp.dma_start(selh[:, :], consts[0:H, K_SELH:K_END]).then_inc(c_in, 16)
            sp.dma_start(vrow[0:8, :], norm_mix_w.rearrange("l (k p) -> (l k) p", p=P)).then_inc(v_in, 16)
            sp.dma_start(vrow[8:16, :], ret_gn_w.rearrange("l (k p) -> (l k) p", p=P)).then_inc(v_in, 16)
            sp.dma_start(vrow[16:24, :], mlstm_gn_w.rearrange("l (k p) -> (l k) p", p=P)).then_inc(v_in, 16)
            sp.dma_start(vrow[24:32, :], conv_b.rearrange("l (k p) -> (l k) p", p=P)).then_inc(v_in, 16)
            sp.dma_start(vrow[32:64, :], conv_w.rearrange("l w o (k p) -> (l w o k) p", p=P)).then_inc(v_in, 16)

            def mix_chunk(n):
                b, half = divmod(n, 2)
                if b < B_WR:
                    w, c0 = w_in[0], IN_COLS[b]
                else:
                    w, c0 = (w_ret, w_mlstm, w_out)[(b - B_WR) // 2][0], 512 * (b % 2)
                if n >= MIX_RAW:
                    sp.wait_ge(wl_ok, 2 * (n - MIX_RAW) + 2)
                sp.dma_start(raw_mix[n % MIX_RAW][:, :, :],
                             w[512 * half:512 * (half + 1), c0:c0 + 512].rearrange("(k p) n -> p k n", p=P))\
                    .then_inc(raw_in[n % MIX_RAW], 16)

            for n in range(MIX_RAW):
                mix_chunk(n)
            sp.wait_ge(vT, 1)
            sp.dma_start(wgr[:, :, :], w_in[0][:, C_IF:C_IF + 2 * H].rearrange("(k p) n -> p k n", p=P)).then_inc(wg_in, 16)
            sp.dma_start(bif[:, 0:1], b_i.rearrange("l h -> h l")).then_inc(wg_in, 16)
            sp.dma_start(bif[:, 1:2], b_f.rearrange("l h -> h l")).then_inc(wg_in, 16)
            for n in range(MIX_RAW, 2 * BLOCKS):
                if n == 2 * B_WM + 2:
                    sp.wait_ge(tr_ps, 2 * KD)
                    sp.dma_start(x2[:, :, :], x[0].rearrange("(t p) d -> p t d", p=P)).then_inc(xr_in, 16)
                    sp.dma_start(wrow[:, :], norm_ffn_w[0:1, :].to_broadcast([P, D])).then_inc(wr_in, 16)
                    sp.dma_start(wrt[:, :, 0:NG], w_group[0].rearrange("(p k) n -> p k n", k=KD)).then_inc(br_in, 16)
                    sp.dma_start(wrt[:, :, NG:36], w_router[0].rearrange("(p k) n -> p k n", k=KD)).then_inc(br_in, 16)
                    sp.dma_start(brt[:, 0:NG], b_group[0:1, :].to_broadcast([P, NG])).then_inc(br_in, 16)
                    sp.dma_start(brt[:, NG:36], b_router[0:1, :].to_broadcast([P, NE])).then_inc(br_in, 16)
                mix_chunk(n)

            def moe_chunk(m, i, used):
                kind, e = stage_of(m // 2)
                e, half, s = i * 2 + e, m % 2, m % MOE_RAW
                if used is not None:
                    sp.wait_ge(wl_ok, used)
                if kind == 2:
                    wd = w_down[0][e] if isinstance(e, int) else w_down[0][bass.ds(e, 1)].rearrange("a f d -> (a f) d")
                    sp.dma_start(raw_moe[s][:, :, :].rearrange("p (f c) n -> p f (c n)", f=2),
                                 wd.rearrange("(p f) n -> p f n", f=KF)[:, 2 * half:2 * half + 2, :]).then_inc(moe_in[s], 16)
                else:
                    w = (w_gate, w_up)[kind][0]
                    wg = w[e] if isinstance(e, int) else w[bass.ds(e, 1)].rearrange("a f d -> (a f) d")
                    sp.dma_start(raw_moe[s][:, :, :],
                                 wg.rearrange("(p k) n -> p k n", k=KD)[:, 4 * half:4 * half + 4, :]).then_inc(moe_in[s], 16)

            def round_chunks(r):
                last = R_PAIRS // 2 - MOE_RAW

                def used(m):
                    return r * R_PAIRS + (MIX_PAIRS + 2 * (m - MOE_RAW) + 2)
                if not isinstance(r, int):
                    for m in range(MOE_RAW):
                        moe_chunk(m, 0, used(m))
                with sp.Fori(0, last // MOE_RAW - 1, 1) as i:
                    for m in range(MOE_RAW, 2 * MOE_RAW):
                        moe_chunk(m, i, i * (2 * MOE_RAW) + used(m))
                for m in range(last, last + MOE_RAW):
                    moe_chunk(m, 0, used(m))

            sp.wait_ge(mo_v, 8)
            moe_chunk(0, 0, None)
            moe_chunk(1, 0, None)
            sp.wait_ge(full[3], B_WO)
            for m in range(2, 6):
                moe_chunk(m, 0, None)
            sp.wait_ge(mgl_ok, KD)
            moe_chunk(6, 0, None)
            moe_chunk(7, 0, None)
            sp.wait_ge(full[3], BLOCKS)
            for m in range(8, MOE_RAW):
                moe_chunk(m, 0, None)
            round_chunks(0)
            sp.wait_ge(cnt_ok, 1)
            most = sp.value_load(cnt[0:1, 0:1], min_val=0, max_val=T)
            with sp.Fori(1, ROUNDS, 1) as r:
                with sp.If(most > r * CAP):
                    round_chunks(r)

            sp.wait_ge(scat_ok, 1)
            for t in range(TT):
                for k in range(2):
                    sp.dma_start(yin[k][:, t, :], y_dram[k * T + t * P:k * T + (t + 1) * P, :]).then_inc(y_in[t], 16)
            for t in range(TT):
                sp.wait_ge(fin_ok, t + 1)
                sp.dma_start(out[0][t * P:(t + 1) * P, :], x2[:, t, :]).then_inc(out_in, 16)
            sp.wait_ge(out_in, 16 * TT)

        @block.tensor
        def _(pe):
            def turn(o, i, k=P):
                return nc.tensor.transpose(o, i, kc[0:k, K_IDENT:K_IDENT + k])

            pe.wait_ge(c_in, 32)
            pe.wait_ge(v_in, 80)
            turn(cb[:, 3, 0:64], vrow[:, :], 64).then_inc(vT, 1)
            pe.wait_ge(xs_ok, TT)
            for k in range(KD):
                if k >= 4:
                    pe.wait_ge(hTl_ok, k - 3)
                elif k == 3:
                    pe.wait_ge(vC, 1)
                for t in range(TT):
                    m = turn(cb[:, k % 4, t * P:(t + 1) * P], xs0[:, t, k * P:(k + 1) * P])
                m.then_inc(hT_ps, 1)
            pe.wait_ge(hTl_ok, KD)

            def mix_half(b, j, half, ah, al):
                s = j % RING
                if half == 0:
                    pe.wait_ge(wl_ok, 4 * b + j + 1)
                for i in (2 * half, 2 * half + 1):
                    if j == 0 and b > 0:
                        pe.wait_ge(free[i], b)
                    cols = slice(i * P, (i + 1) * P)
                    for kk in range(2):
                        k = 2 * j + kk
                        if b in CHANNEL_MAJOR:
                            ops = ((wh[:, s, kk, cols], ah[:, k, :]), (wh[:, s, kk, cols], al[:, k, :]), (wl[:, s, kk, cols], ah[:, k, :]))
                        else:
                            ops = ((ah[:, k, cols], wh[:, s, kk, :]), (al[:, k, cols], wh[:, s, kk, :]), (ah[:, k, cols], wl[:, s, kk, :]))
                        for n, (lhsT, rhs) in enumerate(ops):
                            m = nc.tensor.matmul(pj[:, i, :], lhsT, rhs, start=k == 0 and n == 0, stop=k == KD - 1 and n == 2)
                    if j == 3:
                        m.then_inc(full[i], 1)
                    elif i == 3:
                        m.then_inc(pair_used, 1)

            def ret_scores(c, h):
                i, cs = 4 * c + h, slice(c * P, (c + 1) * P)
                if i == 0:
                    pe.wait_ge(rqT_ok, TT)
                    pe.wait_ge(rkT_ok, TT)
                    pe.wait_ge(gb_ok, H)
                elif i >= 2:
                    pe.wait_ge(r_out, i - 1)
                nc.tensor.matmul(cb[:, i % 2, 0:P], rkT[:, h, cs], rqT[:, h, cs], start=True, stop=True).then_inc(r_s, 1)

            def ret_products(c, h):
                i, cs, hv = 4 * c + h, slice(c * P, (c + 1) * P), slice(h * DV, (h + 1) * DV)
                pe.wait_ge(r_st, i + 1)
                m = nc.tensor.matmul(cb[:, i % 2, P:P + DV], st[:, i % 2, :], rvo[:, c, hv], start=True, stop=c == 0)
                if c > 0:
                    pe.wait_ge(r_R, i - 3)
                    m = nc.tensor.matmul(cb[:, i % 2, P:P + DV], rqT[:, h, cs], Rst[:, h, :], start=False, stop=True)
                if c < TT - 1:
                    if i >= 2:
                        pe.wait_ge(r_R, i - 1)
                    m = nc.tensor.matmul(cb[:, 2 + i % 2, 0:DV], rkn[:, c, h * P:(h + 1) * P], rvo[:, c, hv], start=True, stop=True)
                m.then_inc(r_o, 1)

            def ml_scores(c, h):
                i, cs = 4 * c + h, slice(c * P, (c + 1) * P)
                if i == 0:
                    pe.wait_ge(r_out, 16)
                    pe.wait_ge(r_R, 12)
                    pe.wait_ge(mqk_ok, 8)
                elif i >= 2:
                    pe.wait_ge(m_h, i - 1)
                    pe.wait_ge(m_C, min(i - 1, 12))
                nc.tensor.matmul(cb[:, i % 2, 0:P], mkT[:, h, cs], mqT[:, h, cs], start=True, stop=True)
                turn(cb[:, 2 + i % 2, 0:P], mkT[:, h, cs]).then_inc(m_s, 1)

            def ml_products(c, h):
                i, cs = 4 * c + h, slice(c * P, (c + 1) * P)
                pe.wait_ge(m_st, i + 1)
                m = nc.tensor.matmul(cb[:, i % 2, P:P + DA], st[:, i % 2, :], mva[:, c, h, :], start=True, stop=c == 0)
                if c > 0:
                    pe.wait_ge(m_C, i - 3)
                    pe.wait_ge(wq_ok, H)
                    m = nc.tensor.matmul(cb[:, i % 2, P:P + DA], gbc[:, h, cs], Cst[:, h, :], start=False, stop=True)
                pe.wait_ge(m_wk, i + 1)
                if c < TT - 1:
                    m = nc.tensor.matmul(cb[:, 2 + i % 2, P:P + DA], wk[:, i % 2, :], mva[:, c, h, :], start=True, stop=True)
                m.then_inc(m_o, 1)

            def turn_out(n, src):
                if n == 0:
                    pe.wait_ge(m_h, 16)
                    pe.wait_ge(ret_ok, 16)
                elif n >= 4:
                    pe.wait_ge(tr_l, n - 3)
                if n in (8, 12):
                    pe.wait_ge(hm_ok, (n - 4) // 4)
                for t in range(TT):
                    m = turn(cb[:, n % 4, t * P:(t + 1) * P], src(t, n % KD))
                m.then_inc(tr_ps, 1)

            for b in range(BLOCKS):
                act = (hTh, hTl) if b < B_WR else (retTh, retTl) if b < B_WM else (mixTh, mixTl) if b < B_WO else (mrgTh, mrgTl)
                if b == B_RK:
                    pe.wait_ge(gwl_ok, 2)
                    for k in range(KD):
                        for n, (w_, a_) in enumerate(((wgh, hTh), (wgh, hTl), (wgl, hTh))):
                            m = nc.tensor.matmul(cb[:, 3, :], w_[:, k, :], a_[:, k, :], start=k == 0 and n == 0, stop=k == KD - 1 and n == 2)
                    m.then_inc(g_ps, 1)
                if b == B_RV + 1:
                    pe.wait_ge(grow_ok, 1)
                    pe.wait_ge(rqT_ok, TT)
                    for a in range(3):
                        for c in range(TT):
                            turn(cb[:, 3, a * 16 + c * 4:a * 16 + c * 4 + 4], grow[:, (3, 2, 4)[a], c * P:(c + 1) * P], H)
                    for h in range(H):
                        sel = selh[:, h * P:(h + 1) * P]
                        nc.tensor.matmul(cb[:, 3, 48 + 4 * h:52 + 4 * h], sel, mprev[:, 0:TT], start=True, stop=True)
                        m = nc.tensor.matmul(cb[:, 3, 64 + 4 * h:68 + 4 * h], sel, grow[:, 4, P - 1:T:P], start=True, stop=True)
                    m.then_inc(gtiny, 1)
                if b == B_WR:
                    pe.wait_ge(tr_l, KD)
                if b == B_WM:
                    pe.wait_ge(tr_l, 2 * KD)
                for j in range(4):
                    if b == B_WO:
                        pe.wait_ge(mgl_ok, 2 * j + 2)
                    mix_half(b, j, 0, *act)
                    if B_MQ <= b < B_RG:
                        ret_scores(b - B_MQ, j)
                    if B_RG <= b < B_GM:
                        ml_scores(b - B_RG, j)
                    if b in (B_GM, B_GM + 1):
                        turn_out(4 * (b - B_GM) + j, lambda t, n: rvo[:, t, n * P:(n + 1) * P])
                    if b in (B_WR, B_WR + 1):
                        turn_out(8 + 4 * (b - B_WR) + j, lambda t, n: mva[:, t, n // 2, (n % 2) * P:(n % 2 + 1) * P])
                    mix_half(b, j, 1, *act)
                    if b == B_RV:
                        pe.wait_ge(rope_ok, j + 1)
                        if j == 3:
                            pe.wait_ge(grow_a, 2)
                        for h in range(H):
                            m = turn(cb[:, j, h * P:(h + 1) * P], rqn[:, j, h * P:(h + 1) * P])
                        m.then_inc(rqT_ps, 1)
                    if b == B_RV + 1:
                        pe.wait_ge(rope_ok, TT + j + 1)
                        if j == 3:
                            pe.wait_ge(gcol_ok, 1)
                        for h in range(H):
                            m = turn(cb[:, j, h * P:(h + 1) * P], rkn[:, j, h * P:(h + 1) * P])
                        m.then_inc(rkT_ps, 1)
                        for h in ((), (0,), (1,), (2, 3))[j]:
                            pe.wait_ge(rkT_ok, h + 1)
                            nc.tensor.matmul(cb[:, h, :], selh[:, h * P:(h + 1) * P], grow[:, 4, :],
                                             start=True, stop=True).then_inc(gb_ps, 1)
                    if B_MQ <= b < B_RG:
                        ret_products(b - B_MQ, j)
                    if B_RG <= b < B_GM:
                        ml_products(b - B_RG, j)

            for k in range(KD):
                if k == 0:
                    pe.wait_ge(tr_l, 2 * KD)
                if k < TT:
                    pe.wait_ge(h2_ok, TT)
                else:
                    pe.wait_ge((h2T_v, h2T_a)[k % 2], (k - 4) // 2 + 1)
                for t in range(TT):
                    m = turn(cb[:, k % 4, t * P:(t + 1) * P], h2[:, t, k * P:(k + 1) * P])
                m.then_inc(h2T_ps, 1)
            pe.wait_ge(h2T_v, KD // 2)
            pe.wait_ge(h2T_a, KD // 2)
            pe.wait_ge(br_in, 64)
            pe.wait_ge(free[0], BLOCKS)
            for t in range(TT):
                for k in range(KD):
                    m = nc.tensor.matmul(pj[:, 0, t * 36:(t + 1) * 36], h2T[:, k, t * P:(t + 1) * P], wrt[:, k, :], start=k == 0, stop=k == KD - 1)
            m.then_inc(lg_ps, 1)
            pe.wait_ge(hot_in, 1)
            pe.wait_ge(free[1], BLOCKS)
            for t in range(TT + 1):
                for t2 in range(min(t + 1, TT)):
                    w_ = kc[:, K_BEFORE:K_BEFORE + P] if t2 == t else onesq[:, :]
                    m = nc.tensor.matmul(pj[:, 1, t * NE:(t + 1) * NE], w_, rt[:, 0, t2 * NE:(t2 + 1) * NE], start=t2 == 0, stop=t2 == min(t, TT - 1))
            m.then_inc(pos_ps, 1)

            def weights_pair(r, i, t, lhs, banks, first, last):
                pe.wait_ge(wl_ok, r * R_PAIRS + i * 24 + (MIX_PAIRS + t + 1))
                one = banks[0] == banks[1]
                for kk in range(2):
                    for n, w_ in enumerate((wh, wl)):
                        m = nc.tensor.matmul(pj[:, banks[kk], :], lhs(kk), w_[:, t % RING, kk, :],
                                             start=first and n == 0 and not (one and kk == 1),
                                             stop=last and n == 1 and not (one and kk == 0))
                return m

            def turn_x(E, par, n):
                if E is not None:
                    pe.wait_ge(xl_ok, E)
                pe.wait_ge(gat[par], n * 16 + 16)
                pe.sem_inc(pe_past, 1)
                for k in range(KD):
                    m = turn(cb[:, 0, k * CAP:(k + 1) * CAP], xg[:, par, k * P:(k + 1) * P], CAP)
                m.then_inc(xT_ps, 1)

            def gate_or_up(r, i, E, par, t, up):
                if not up:
                    pe.wait_ge(xl_ok, E + 1)
                if not isinstance(E, int) or E > 0:
                    pe.wait_ge((gs_ok, us_ok)[up], E)
                for j in range(4):
                    m = weights_pair(r, i, t + j, lambda kk: xsp[par][:, 2 * j + kk, :], (up, up), j == 0, j == 3)
                    m.then_inc((g_f, u_f)[up] if j == 3 else pair_used, 1)

            def turn_gu(E, par):
                pe.wait_ge(gs_ok, E + 1)
                pe.wait_ge(us_ok, E + 1)
                pe.wait_ge(hf_ok, E + 1)
                for a in range(2):
                    for f in range(KF):
                        m = nc.tensor.matmul(cb[:, 1, (a * KF + f) * CAP:(a * KF + f + 1) * CAP], us[:, f, :] if a else gs[:, par, f, :],
                                             kc[:, K_SEL64:K_SEL64 + CAP], start=True, stop=True)
                m.then_inc(gt_ps, 1)

            def down(r, i, E, t):
                pe.wait_ge(hl_ok, E + 1)
                pe.wait_ge(yo_ok, E + 1)
                for j in range(4):
                    m = weights_pair(r, i, t + j, lambda kk: hsp[:, j, :], (2, 3), j == 0, j == 3)
                    m.then_inc(y_f if j == 3 else pair_used, 1)

            def moe_round(r):
                E0, n0 = r * NE, r * (NE // 2)
                pe.wait_ge(hot_ok, r + 1)
                for e in range(NE):
                    for t in range(TT):
                        m = nc.tensor.matmul(cb[0:CAP, 2, 2 * e:2 * e + 2], hot[:, t, e, :], val[:, t, e, :], start=t == 0, stop=t == TT - 1)
                m.then_inc(tab_ps, 1)
                turn_x(None if isinstance(r, int) else E0, 0, n0)
                gate_or_up(r, 0, E0, 0, 0, 0)
                turn_x(E0 + 1, 1, n0)
                gate_or_up(r, 0, E0, 0, 4, 1)

                def expert(i, e, par, t, last):
                    E = E0 + i * 2 + e
                    gate_or_up(r, i, E, par, t, 0)
                    turn_gu(E - 1, 1 - par)
                    if not last:
                        turn_x(E + 1, 1 - par, n0 + i + (e + 1) // 2)
                    gate_or_up(r, i, E, par, t + 4, 1)
                    down(r, i, E - 1, t + 8)

                with pe.Fori(0, NE // 2 - 1, 1) as i:
                    expert(i, 1, 1, 8, False)
                    expert(i, 2, 0, 20, False)
                expert(0, NE - 1, 1, 8 + E_PAIRS * (NE - 2), True)
                turn_gu(E0 + NE - 1, 1)
                down(r, 0, E0 + NE - 1, R_PAIRS - 4)

            moe_round(0)
            pe.wait_ge(cnt_ok, 1)
            most = pe.value_load(cnt[0:1, 0:1], min_val=0, max_val=T)
            with pe.Fori(1, ROUNDS, 1) as r:
                with pe.If(most > r * CAP):
                    moe_round(r)

        @block.scalar
        def _(act):
            chain = [0]

            def own(ins):
                chain[0] += 1
                ins.then_inc(a_own, 1)
                act.wait_ge(a_own, chain[0])

            def mix_head(q):
                n = q // 2
                act.wait_ge(raw_in[n % MIX_RAW], 16 * (n // MIX_RAW + 1))
                if q >= RING:
                    wait_mix_pair(act, q - RING)
                nc.scalar.activation(wh[:, q % RING, :, :], raw_mix[n % MIX_RAW][:, 2 * (q % 2):2 * (q % 2) + 2, :], ACT.Copy).then_inc(wh_ok, 1)

            def root(n, width):
                act.wait_ge(var_ok, n + 1)
                nc.scalar.activation(stat[:, 1, 0:width], stat[:, 0, 0:width], ACT.Sqrt).then_inc(root_ok, 1)

            act.wait_ge(x_in, 16)
            for t in range(TT):
                nc.scalar.activation(rvo[:, t, :], xt[:, t, :], ACT.Square, accum_out=ssq[:, t:t + 1]).then_inc(sq_ok, 1)
            for q in range(LEAD):
                mix_head(q)
            root(0, TT)
            act.wait_ge(vC, 1)
            for k in range(KD):
                act.wait_ge(hT_ps, k + 1)
                nc.scalar.activation(hTh[:, k, :], cb[:, k % 4, :], ACT.Identity, scale=vcol[:, k:k + 1]).then_inc(hTh_ok, 1)
            act.wait_ge(wg_in, 48)
            act.wait_ge(zero_ok, 3)
            for a in range(2):
                nc.scalar.activation(wgh[:, :, 32 * a:32 * a + H], wgr[:, :, H * a:H * a + H], ACT.Copy).then_inc(gwh_ok, 1)

            def bank_copy(b, i, dst):
                act.wait_ge(full[i], b + 1)
                nc.scalar.activation(dst, pj[:, i, :], ACT.Copy).then_inc(free[i], 1)

            def ret_output(i):
                c, h = divmod(i, 4)
                act.wait_ge(r_o, i + 1)
                if i >= 1:
                    act.wait_ge(r_out, i)
                nc.scalar.activation(rsq[:, :], cb[:, i % 2, P:P + DV], ACT.Square, accum_out=ssq[:, i:i + 1])
                nc.scalar.activation(rvo[:, c, h * DV:(h + 1) * DV], cb[:, i % 2, P:P + DV], ACT.Copy).then_inc(r_out, 1)

            def ml_output(i):
                c, h = divmod(i, 4)
                act.wait_ge(m_rc, i + 1)
                nc.scalar.activation(mva[:, c, h, 0:DV], cb[:, i % 2, P:P + DV], ACT.Copy, scale=rden[:, i % 2:i % 2 + 1]).then_inc(m_h, 1)

            def out_head(n):
                act.wait_ge(tr_ps, n + 1)
                if n == KD:
                    wait_mix_pair(act, 4 * B_WR - 1)
                nc.scalar.activation((retTh, mixTh)[n // KD][:, n % KD, :], cb[:, n % 4, :], ACT.Identity, scale=vcol[:, 8 + n:9 + n]).then_inc(tr_h, 1)

            for b in range(BLOCKS + 1):
                p = b - 1
                for i in range(4):
                    if p == B_RQ:
                        bank_copy(p, i, rqn[:, i, :])
                    if p == B_RK:
                        bank_copy(p, i, rkn[:, i, :])
                    if p in (B_RV, B_RV + 1):
                        bank_copy(p, i, rvo[:, i, 512 * (p - B_RV):512 * (p - B_RV + 1)])
                    if p in (B_MQ, B_MK):
                        if p == B_MQ and i == 0:
                            act.wait_ge(zero_ok, 3)
                        if p == B_MK:
                            act.wait_ge(mqk_ok, i + 1)
                        bank_copy(p, i, convx[:, i, 3:3 + T])
                    if p in (B_MV, B_MV + 1):
                        h0 = 2 * (p - B_MV)
                        act.wait_ge(full[i], p + 1)
                        nc.scalar.activation(mva[:, i, h0:h0 + 2, 0:DV], pj[:, i, :].rearrange("p (h v) -> p h v", h=2), ACT.Copy).then_inc(free[i], 1)
                    if p in (B_RG, B_RG + 1):
                        n = 4 * (p - B_RG) + i
                        act.wait_ge(full[i], p + 1)
                        if n >= 2:
                            act.wait_ge(ret_ok, 2 * (n - 1))
                        nc.scalar.activation(rsg[:, n % 2, :], pj[:, i, :], ACT.Sigmoid).then_inc(rg_s, 1)
                    if p in (B_GR, B_GR + 1, B_GM, B_GM + 1):
                        dst, ct = (mrg, 4 * (p - B_GR) + i) if p < B_GM else (sgm, 4 * (p - B_GM) + i)
                        act.wait_ge(full[i], p + 1)
                        if p == B_GR and i == 0:
                            act.wait_ge(ret_ok, 16)
                        nc.scalar.activation(dst[:, ct, :], pj[:, i, :], ACT.Sigmoid).then_inc(free[i], 1)
                    if p in (B_MO, B_MO + 1):
                        n = 4 * (p - B_MO) + i
                        act.wait_ge(full[i], p + 1)
                        if n == 0:
                            act.wait_ge(tr_ps, KD)
                        if n >= 2:
                            act.wait_ge(mo_v, n - 1)
                        nc.scalar.activation(msg[:, n % 2, :], pj[:, i, :], ACT.Sigmoid).then_inc(free[i], 1)
                    if p in (B_WM, B_WM + 1):
                        ct = 4 * (p - B_WM) + i
                        act.wait_ge(mg_ok, ct + 1)
                        if ct == 0:
                            wait_mix_pair(act, 4 * B_WM - 1)
                        nc.scalar.activation(mrgTh[:, ct, :], mrg[:, ct, :], ACT.Copy).then_inc(mgh_ok, 1)
                if b == BLOCKS:
                    break
                if b == B_RV:
                    act.wait_ge(g_ps, 1)
                    nc.scalar.activation(grow[:, 0, :], cb[0:H, 3, :], ACT.Identity, bias=bif[:, 0:1]).then_inc(grow_a, 1)
                    nc.scalar.activation(grow[:, 1, :], cb[32:32 + H, 3, :], ACT.Copy).then_inc(grow_a, 1)
                    act.wait_ge(f_abs, 1)
                    own(nc.scalar.activation(grow[:, 2, :], grow[:, 2, :], ACT.Exp, scale=-1.0))
                    nc.scalar.activation(grow[:, 2, :], grow[:, 2, :], ACT.Ln, bias=1.0).then_inc(f_log, 1)
                if b == B_MQ:
                    act.wait_ge(gex_in, 1)
                    nc.scalar.activation(gex[:, :, :], gex[:, :, :], ACT.Exp).then_inc(gex_ok, 1)
                if b == B_RG:
                    ret_output(15)
                    root(1, 16)
                for j in range(4):
                    q = 4 * b + j
                    i = 4 * (b - B_MQ) + j
                    if 0 < i < 16:
                        ret_output(i - 1)
                    i = 4 * (b - B_RG) + j
                    if 0 < i < 17:
                        ml_output(i - 1)
                    if q + LEAD < MIX_PAIRS:
                        mix_head(q + LEAD)
                    if b == B_RV + 1:
                        act.wait_ge(rkT_ps, j + 1)
                        nc.scalar.activation(rkT[:, :, j * P:(j + 1) * P], cb[:, j, :].rearrange("p (h l) -> p h l", h=H), ACT.Copy).then_inc(rkT_ok, 1)
                        for h in ((), (0,), (1,), (2, 3))[j]:
                            act.wait_ge(gb_ps, h + 1)
                            nc.scalar.activation(gbc[:, h, :], cb[:, h, :], ACT.Copy).then_inc(gb_ok, 1)
                    if b == B_MQ:
                        act.wait_ge(dt_in, j + 1)
                        nc.scalar.activation(dT[:, j, :], dT[:, j, :], ACT.Exp, scale=-1.0).then_inc(dt_ok, 1)
                        for c in range(TT):
                            m = nc.scalar.activation(gbc[:, j, c * P:(c + 1) * P], gbc[:, j, c * P:(c + 1) * P], ACT.Exp, scale=-1.0,
                                                     bias=gcol[:, 3, 4 * j + c:4 * j + c + 1])
                        m.then_inc(wint_ok, 1)
                    if b in (B_MQ + 1, B_MK + 1):
                        n = 4 * (b - B_MQ - 1) + j
                        dst = (mqT, mkT)[n // 4]
                        act.wait_ge(free[j], b)
                        nc.scalar.activation(dst[:, j, :], convx[:, j, 3:3 + T], ACT.Identity, scale=vcol[:, 56 + n:57 + n], bias=vcol[:, 24 + n:25 + n]).then_inc(conv_a, 1)
                        act.wait_ge(conv_v, n + 1)
                        if n >= 1:
                            act.wait_ge(mqk_ok, n)
                        nc.scalar.activation(csg[:, :], dst[:, j, :], ACT.Sigmoid).then_inc(conv_s, 1)
                    if B_RG <= b < B_GM:
                        i = 4 * (b - B_RG) + j
                        act.wait_ge(m_s, i + 1)
                        if i >= 2:
                            act.wait_ge(m_o, i - 1)
                        nc.scalar.activation(wk[:, i % 2, :], cb[:, 2 + i % 2, 0:P], ACT.Copy, scale=gex[:, 1, i:i + 1]).then_inc(m_wk, 1)
                    if b in (B_MO + 1, B_MO + 2):
                        n = 4 * (b - B_MO - 1) + j
                        act.wait_ge(mo_v, n + 1)
                        h = 2 * (b - B_MO - 1)
                        for a in range(2):
                            m = nc.scalar.activation(rsq[:, :], mva[:, j, h + a, 0:DV], ACT.Square, accum_out=ssq[:, 4 * (h + a) + j:4 * (h + a) + j + 1])
                            if a == 0:
                                own(m)
                        m.then_inc(sq_ok, 1)
                        act.wait_ge(sq_ok, TT + n + 1)
                    if b in (B_GM, B_GM + 1):
                        out_head(4 * (b - B_GM) + j)
                    if b in (B_WR, B_WR + 1):
                        out_head(8 + 4 * (b - B_WR) + j)
                    if b in (B_MO + 1, B_MO + 2) and j == 3:
                        root(2 + b - B_MO - 1, 8)

            for t in range(TT):
                act.wait_ge(free[t], BLOCKS)
                nc.scalar.activation(h2[:, t, :], x2[:, t, :], ACT.Square, accum_out=ssq[:, t:t + 1]).then_inc(sq_ok, 1)
            root(4, TT)
            for t in range(TT):
                act.wait_ge(h2_ok, t + 1)
                act.dma_start(h_dram[t * P:(t + 1) * P, :], h2[:, t, :]).then_inc(h2_out, 16)
            act.dma_start(wrow[:, :], norm_final_w.rearrange("(a d) -> a d", a=1).to_broadcast([P, D])).then_inc(wr_in, 16)
            for k in range(1, KD, 2):
                act.wait_ge(h2T_ps, k + 1)
                nc.scalar.activation(h2T[:, k, :], cb[:, k % 4, :], ACT.Copy).then_inc(h2T_a, 1)
            act.wait_ge(e1_in, 1)
            nc.scalar.activation(rt[:, 5, 0:TT * NG], rt[:, 5, 0:TT * NG], ACT.Exp).then_inc(e1_ok, 1)
            act.wait_ge(e2_in, 1)
            nc.scalar.activation(rt[:, 6, 0:TT], rt[:, 6, 0:TT], ACT.Exp).then_inc(e2_ok, 1)

            def head(r, i, t):
                src, s, loads = moe_raw(t)
                act.wait_ge(moe_in[s], r * (16 * LOADS) + i * 16 + 16 * loads)
                wait_pair_used(act, r, i, t)
                nc.scalar.activation(wh[:, t % RING, :, :], src, ACT.Copy).then_inc(wh_ok, 1)

            def x_head(E, par):
                act.wait_ge(xT_ps, E + 1)
                nc.scalar.activation(xsp[par][:, :, 0:CAP], cb[:, 0, :].rearrange("p (k n) -> p k n", k=KD), ACT.Copy).then_inc(xh_ok, 1)

            def gate_copy(E, par):
                act.wait_ge(g_f, E + 1)
                nc.scalar.activation(gs[:, par, :, :], pj[:, 0, :].rearrange("p (m f) -> p f m", f=KF), ACT.Copy).then_inc(gs_ok, 1)

            def gate_sigmoid(E):
                act.wait_ge(gt_ps, E + 1)
                nc.scalar.activation(sg[:, :], cb[:, 1, 0:KF * CAP], ACT.Sigmoid).then_inc(sg_ok, 1)

            def hidden_head(E):
                act.wait_ge(hf_ok, E + 2)
                nc.scalar.activation(hsp[:, :, 0:CAP], hf[:, :].rearrange("p (f n) -> p f n", f=KF), ACT.Copy).then_inc(hh_ok, 1)

            def y_tails(E):
                act.wait_ge(y_f, E + 1)
                act.wait_ge(yo_ok, E + 1)
                nc.scalar.activation(yb[:, :].rearrange("p (a n) -> p a n", a=2), pj[CAP:P, 2:4, :], ACT.Copy).then_inc(yb_ok, 1)

            def moe_round(r):
                E0 = r * NE
                for t in range(LEAD):
                    head(r, 0, t)
                x_head(E0, 0)
                for t in range(8):
                    head(r, 0, t + LEAD)
                    if t == 4:
                        gate_copy(E0, 0)
                        x_head(E0 + 1, 1)

                def expert(i, e, par, t, last):
                    E = E0 + i * 2 + e
                    for s in range(E_PAIRS):
                        head(r, i, t + s + LEAD)
                        if s == 4:
                            gate_copy(E, par)
                            gate_sigmoid(E - 1)
                        if s == 5 and not last:
                            x_head(E + 1, 1 - par)
                        if s == 5:
                            hidden_head(E - 1)
                    y_tails(E - 1)

                with act.Fori(0, NE // 2 - 1, 1) as i:
                    expert(i, 1, 1, 8, False)
                    expert(i, 2, 0, 20, False)
                expert(0, NE - 1, 1, 8 + E_PAIRS * (NE - 2), True)
                head(r, 0, R_PAIRS - 1)
                gate_sigmoid(E0 + NE - 1)
                hidden_head(E0 + NE - 1)
                y_tails(E0 + NE - 1)

            moe_round(0)
            act.wait_ge(cnt_ok, 1)
            most = act.value_load(cnt[0:1, 0:1], min_val=0, max_val=T)
            with act.Fori(1, ROUNDS, 1) as r:
                with act.If(most > r * CAP):
                    moe_round(r)

            for t in range(TT):
                act.wait_ge(x3_ok, t + 1)
                nc.scalar.activation(yin[0][:, t, :], x2[:, t, :], ACT.Square, accum_out=ssq[:, t:t + 1]).then_inc(sq_ok, 1)
            root(5, TT)

        @block.vector
        def _(dve):
            chain = [0]

            def own(ins):
                chain[0] += 1
                ins.then_inc(v_own, 1)
                dve.wait_ge(v_own, chain[0])

            V = nc.vector

            def mix_tail(q):
                dve.wait_ge(wh_ok, q + 1)
                n = q // 2
                V.tensor_tensor(wl[:, q % RING, :, :], raw_mix[n % MIX_RAW][:, 2 * (q % 2):2 * (q % 2) + 2, :],
                                wh[:, q % RING, :, :].bitcast(F32), ALU.subtract).then_inc(wl_ok, 1)

            def rstd(n, squares, width, dim):
                v, s, y, z = (stat[:, a, 0:width] for a in range(4))
                V.tensor_scalar(v, squares, 1.0 / dim, EPS, ALU.mult, ALU.add).then_inc(var_ok, 1)
                dve.wait_ge(root_ok, n + 1)
                own(V.reciprocal(y, s))
                own(V.tensor_tensor(z, y, y, ALU.mult))
                dve.wait_ge(var_ok, n + 1)
                own(V.tensor_tensor(z, z, v, ALU.mult))
                own(V.tensor_scalar(z, z, -0.5, 1.5, ALU.mult, ALU.add))
                own(V.tensor_tensor(y, y, z, ALU.mult))

            dve.wait_ge(sq_ok, TT)
            rstd(0, ssq[:, 0:TT], TT, D)
            for t in range(TT):
                V.tensor_scalar(xs0[:, t, :], xt[:, t, :], stat[:, 2, t:t + 1], None, ALU.mult).then_inc(xs_ok, 1)
            dve.wait_ge(vT, 1)
            V.tensor_copy(vcol[:, :], cb[:, 3, 0:64]).then_inc(vC, 1)
            dve.wait_ge(vC, 1)
            for k in range(KD):
                dve.wait_ge(hTh_ok, k + 1)
                V.scalar_tensor_tensor(hTl[:, k, :], cb[:, k % 4, :], vcol[:, k:k + 1], hTh[:, k, :].bitcast(F32), ALU.mult, ALU.subtract).then_inc(hTl_ok, 1)
                if k in (1, 3, 5):
                    mix_tail(k // 2)
            for a in range(2):
                dve.wait_ge(gwh_ok, a + 1)
                V.tensor_tensor(wgl[:, :, 32 * a:32 * a + H], wgr[:, :, H * a:H * a + H], wgh[:, :, 32 * a:32 * a + H].bitcast(F32), ALU.subtract).then_inc(gwl_ok, 1)

            def rotate(t, src, done):
                if done:
                    dve.wait_ge(rope_ok, done)
                xx = src[:, t, :].rearrange("p (h a d) -> p h a d", h=H, a=2)
                cos = kc[:, K_COS + 64 * t:K_COS + 64 * (t + 1)].unsqueeze(1)
                sin = kc[:, K_SIN + 64 * t:K_SIN + 64 * (t + 1)].unsqueeze(1).to_broadcast([P, H, 64])
                a_ = rtmp[:, 0, :].rearrange("p (h a d) -> p h a d", h=H, a=2)
                b_ = rtmp[:, 1, :].rearrange("p (h a d) -> p h a d", h=H, a=2)
                V.tensor_tensor(rtmp[:, 0, :].rearrange("p (g d) -> p g d", d=64), src[:, t, :].rearrange("p (g d) -> p g d", d=64),
                                cos.to_broadcast([P, 2 * H, 64]), ALU.mult)
                V.tensor_tensor(b_[:, :, 0, :], xx[:, :, 1, :], sin, ALU.mult)
                own(V.tensor_tensor(b_[:, :, 1, :], xx[:, :, 0, :], sin, ALU.mult))
                V.tensor_tensor(xx[:, :, 0, :], a_[:, :, 0, :], b_[:, :, 0, :], ALU.subtract)
                last = V.tensor_tensor(xx[:, :, 1, :], a_[:, :, 1, :], b_[:, :, 1, :], ALU.add)
                return last

            def rq_turned(t):
                dve.wait_ge(rqT_ps, t + 1)
                V.tensor_tensor(rqT[:, :, t * P:(t + 1) * P], cb[:, t, :].rearrange("p (h l) -> p h l", h=H),
                                kc[:, K_QDEC:K_QDEC + H * P].rearrange("p (h l) -> p h l", h=H), ALU.mult).then_inc(rqT_ok, 1)

            def ret_masked(i):
                dve.wait_ge(r_s, i + 1)
                V.tensor_tensor(st[:, i % 2, :], cb[:, i % 2, 0:P], kc[:, K_RMASK + (i % 4) * P:K_RMASK + (i % 4 + 1) * P], ALU.mult).then_inc(r_st, 1)

            def ret_state(i):
                c, h = divmod(i, 4)
                if c == TT - 1:
                    return
                dve.wait_ge(r_o, i + 1)
                if c == 0:
                    V.tensor_copy(Rst[:, h, :], cb[:, 2 + i % 2, 0:DV]).then_inc(r_R, 1)
                else:
                    V.scalar_tensor_tensor(Rst[:, h, :], Rst[:, h, :], GAMMA[h] ** P, cb[:, 2 + i % 2, 0:DV], ALU.mult, ALU.add).then_inc(r_R, 1)

            def ml_weighted(i):
                c, h = divmod(i, 4)
                dve.wait_ge(m_s, i + 1)
                V.tensor_tensor(st[:, i % 2, :], cb[:, i % 2, 0:P], dT[:, h, c * P:(c + 1) * P], ALU.mult).then_inc(m_st, 1)

            def ml_state(i):
                c, h = divmod(i, 4)
                dve.wait_ge(m_o, i + 1)
                if i >= 2:
                    dve.wait_ge(m_h, i - 1)
                den, tmp = cb[:, i % 2, P + DV:P + DA], rden[:, i % 2:i % 2 + 1]
                own(V.tensor_scalar(tmp, den, -1.0, gex[:, 0, i:i + 1], ALU.mult, ALU.max))
                own(V.tensor_tensor(tmp, den, tmp, ALU.max))
                V.reciprocal(tmp, tmp).then_inc(m_rc, 1)
                if c == 0:
                    V.tensor_copy(Cst[:, h, :], cb[:, 2 + i % 2, P:P + DA]).then_inc(m_C, 1)
                elif c < TT - 1:
                    V.scalar_tensor_tensor(Cst[:, h, :], Cst[:, h, :], gex[:, 2, i:i + 1], cb[:, 2 + i % 2, P:P + DA], ALU.mult, ALU.add).then_inc(m_C, 1)

            def out_tail(n):
                dve.wait_ge(tr_h, n + 1)
                V.scalar_tensor_tensor((retTl, mixTl)[n // KD][:, n % KD, :], cb[:, n % 4, :], vcol[:, 8 + n:9 + n],
                                       (retTh, mixTh)[n // KD][:, n % KD, :].bitcast(F32), ALU.mult, ALU.subtract).then_inc(tr_l, 1)

            for b in range(BLOCKS + 1):
                p = b - 1
                for i in range(4):
                    if p in (B_RG, B_RG + 1):
                        n = 4 * (p - B_RG) + i
                        dve.wait_ge(rg_s, n + 1)
                        V.tensor_tensor(rsg[:, n % 2, :], pj[:, i, :], rsg[:, n % 2, :], ALU.mult).then_inc(free[i], 1)
                        dve.wait_ge(free[i], p + 1)
                        for a in range(2):
                            h = 2 * (p - B_RG) + a
                            V.scalar_tensor_tensor(rvo[:, i, h * DV:(h + 1) * DV], rvo[:, i, h * DV:(h + 1) * DV], rret[:, 4 * i + h:4 * i + h + 1],
                                                   rsg[:, n % 2, a * DV:(a + 1) * DV], ALU.mult, ALU.mult).then_inc(ret_ok, 1)
                    if p in (B_MO, B_MO + 1):
                        n, h0 = 4 * (p - B_MO) + i, 2 * (p - B_MO)
                        dve.wait_ge(free[i], p + 1)
                        V.tensor_tensor(mva[:, i, h0:h0 + 2, 0:DV], mva[:, i, h0:h0 + 2, 0:DV],
                                        msg[:, n % 2, :].rearrange("p (h v) -> p h v", h=2), ALU.mult).then_inc(mo_v, 1)
                    if p in (B_WR, B_WR + 1):
                        ct = 4 * (p - B_WR) + i
                        dve.wait_ge(full[i], p + 1)
                        V.tensor_tensor(mrg[:, ct, :], pj[:, i, :], mrg[:, ct, :], ALU.mult).then_inc(free[i], 1)
                    if p in (B_WM, B_WM + 1):
                        ct = 4 * (p - B_WM) + i
                        dve.wait_ge(full[i], p + 1)
                        V.tensor_tensor(sgm[:, ct, :], pj[:, i, :], sgm[:, ct, :], ALU.mult).then_inc(free[i], 1)
                        dve.wait_ge(free[i], p + 1)
                        V.tensor_tensor(mrg[:, ct, :], mrg[:, ct, :], sgm[:, ct, :], ALU.add).then_inc(mg_ok, 1)
                        dve.wait_ge(mgh_ok, ct + 1)
                        V.tensor_tensor(mrgTl[:, ct, :], mrg[:, ct, :], mrgTh[:, ct, :].bitcast(F32), ALU.subtract).then_inc(mgl_ok, 1)
                    if p in (B_WO, B_WO + 1):
                        half = slice(512 * (p - B_WO), 512 * (p - B_WO + 1))
                        if p == B_WO and i == 0:
                            dve.wait_ge(xr_in, 16)
                        dve.wait_ge(full[i], p + 1)
                        V.tensor_tensor(x2[:, i, half], pj[:, i, :], x2[:, i, half], ALU.add).then_inc(free[i], 1)
                if b == BLOCKS:
                    break
                if b == B_RV:
                    dve.wait_ge(grow_a, 2)
                    own(V.tensor_scalar(grow[:, 1, :], grow[:, 1, :], bif[:, 1:2], None, ALU.add))
                    V.scalar_tensor_tensor(grow[:, 2, :], grow[:, 1, :], -1.0, grow[:, 1, :], ALU.mult, ALU.max).then_inc(f_abs, 1)
                    dve.wait_ge(f_log, 1)
                    own(V.scalar_tensor_tensor(grow[:, 1, :], grow[:, 1, :], 0.0, grow[:, 2, :], ALU.min, ALU.subtract))
                    for c in range(TT):
                        cs = slice(c * P, (c + 1) * P)
                        m = V.tensor_tensor_scan(grow[:, 2, cs], onesq[0:H, :], grow[:, 1, cs], 0.0, ALU.mult, ALU.add)
                    own(m)
                    own(V.tensor_tensor(grow[:, 3, :], grow[:, 0, :], grow[:, 2, :], ALU.subtract))
                    own(V.memset(mprev[:, 0:1], 0.0))
                    for c in range(TT):
                        cs, end = slice(c * P, (c + 1) * P), (c + 1) * P - 1
                        own(V.tensor_tensor_scan(grow[:, 4, cs], grow[:, 3, cs], grow[:, 3, cs], mprev[:, c:c + 1], ALU.max, ALU.max))
                        m = V.tensor_tensor(mprev[:, c + 1:c + 2], grow[:, 2, end:end + 1], grow[:, 4, end:end + 1], ALU.add)
                        if c < TT - 1:
                            own(m)
                    m.then_inc(grow_ok, 1)
                if b == B_RV + 1:
                    dve.wait_ge(gtiny, 1)
                    V.tensor_copy(gcol[:, :, :], cb[:, 3, 0:80].rearrange("p (a n) -> p a n", a=5)).then_inc(gcol_ok, 1)
                    dve.wait_ge(gcol_ok, 1)
                    last = gcol[:, 4, :].rearrange("p (h c) -> p c h", h=H)
                    V.scalar_tensor_tensor(gex[:, 0, :], gcol[:, 1, :], -1.0, gcol[:, 2, :], ALU.mult, ALU.subtract)
                    V.tensor_tensor(gex[:, 1, :].rearrange("p (c h) -> p c h", h=H), gcol[:, 0, :].rearrange("p (c h) -> p c h", h=H), last, ALU.subtract)
                    V.tensor_tensor(gex[:, 2, :].rearrange("p (c h) -> p c h", h=H), gcol[:, 3, :].rearrange("p (h c) -> p c h", h=H), last, ALU.subtract).then_inc(gex_in, 1)
                if b == B_RG:
                    dve.wait_ge(r_out, 16)
                    rstd(1, ssq[:, :], 16, DV)
                    own(V.tensor_copy(rret[:, :], stat[:, 2, :]))
                    dve.wait_ge(gex_ok, 1)
                for j in range(4):
                    q = 4 * b + j
                    i = 4 * (b - B_MQ) + j
                    if 0 < i < 16:
                        ret_state(i - 1)
                    i = 4 * (b - B_RG) + j
                    if 0 < i < 17:
                        ml_state(i - 1)
                    if q + LEAD < MIX_PAIRS:
                        mix_tail(q + LEAD)
                    if b == B_RK:
                        dve.wait_ge(free[j], B_RQ + 1)
                        rotate(j, rqn, j).then_inc(rope_ok, 1)
                    if b == B_RV:
                        if j >= 1:
                            rq_turned(j - 1)
                        dve.wait_ge(free[j], B_RK + 1)
                        own(rotate(j, rkn, TT + j))
                        kk = rkn[:, j, :].rearrange("p (h d) -> p h d", h=H)
                        V.tensor_tensor(kk, kk, kc[:, K_KDEC:K_KDEC + H].unsqueeze(2).to_broadcast([P, H, DK]), ALU.mult).then_inc(rope_ok, 1)
                    if b == B_MQ:
                        dve.wait_ge(gb_ok, j + 1)
                        for c in range(TT):
                            m = V.scalar_tensor_tensor(dT[:, j, c * P:(c + 1) * P], gbc[:, j, c * P:(c + 1) * P], gcol[:, 0, 4 * c + j:4 * c + j + 1],
                                                       kc[:, K_NOTYET:K_NOTYET + P], ALU.subtract, ALU.add)
                        m.then_inc(dt_in, 1)
                    if B_MQ <= b < B_RG:
                        ret_masked(4 * (b - B_MQ) + j)
                    if b in (B_MQ + 1, B_MK + 1):
                        n = 4 * (b - B_MQ - 1) + j
                        dst = (mqT, mkT)[n // 4][:, j, :]
                        dve.wait_ge(conv_a, n + 1)
                        for tap in range(3):
                            m = V.scalar_tensor_tensor(dst, convx[:, j, tap:tap + T], vcol[:, 32 + 8 * tap + n:33 + 8 * tap + n], dst, ALU.mult, ALU.add)
                            if tap < 2:
                                own(m)
                        m.then_inc(conv_v, 1)
                        dve.wait_ge(conv_s, n + 1)
                        V.scalar_tensor_tensor(dst, dst, (1.0, DK ** -0.5)[n // 4], csg[:, :], ALU.mult, ALU.mult).then_inc(mqk_ok, 1)
                    if b == B_MV + 1:
                        if j == 0:
                            dve.wait_ge(mqk_ok, 8)
                        dve.wait_ge(wint_ok, j + 1)
                        V.tensor_tensor(gbc[:, j, :], gbc[:, j, :], mqT[:, j, :], ALU.mult).then_inc(wq_ok, 1)
                    if B_RG <= b < B_GM:
                        if b == B_RG and j == 0:
                            dve.wait_ge(dt_ok, H)
                        ml_weighted(4 * (b - B_RG) + j)
                    if b in (B_GM, B_GM + 1):
                        out_tail(4 * (b - B_GM) + j)
                    if b in (B_WR, B_WR + 1):
                        out_tail(8 + 4 * (b - B_WR) + j)
                    if b in (B_MO + 1, B_MO + 2) and j == 3:
                        half = b - B_MO - 1
                        dve.wait_ge(sq_ok, TT * (2 + half))
                        rstd(2 + half, ssq[:, 8 * half:8 * half + 8], 8, DV)
                        for t in range(TT):
                            for a in range(2):
                                hv = mva[:, t, 2 * half + a, 0:DV]
                                m = V.tensor_scalar(hv, hv, stat[:, 2, 4 * a + t:4 * a + t + 1], None, ALU.mult)
                        m.then_inc(hm_ok, 1)
                if b == B_RV:
                    rq_turned(3)

            dve.wait_ge(sq_ok, 4 * TT)
            rstd(4, ssq[:, 0:TT], TT, D)
            dve.wait_ge(wr_in, 16)
            for t in range(TT):
                V.scalar_tensor_tensor(h2[:, t, :].rearrange("q (k p) -> q k p", k=KD), x2[:, t, :].rearrange("q (p k) -> q k p", k=KD), stat[:, 2, t:t + 1],
                                       wrow[:, :].rearrange("q (p k) -> q k p", k=KD), ALU.mult, ALU.mult).then_inc(h2_ok, 1)
            for k in range(0, KD, 2):
                dve.wait_ge(h2T_ps, k + 1)
                V.tensor_copy(h2T[:, k, :], cb[:, k % 4, :]).then_inc(h2T_v, 1)

            def tiles(a, n):
                return rt[:, a, 0:TT * n].rearrange("p (t n) -> p t n", n=n)

            def first_best(score, best, n, a_, b_):
                x_, y_ = tiles(a_, n), rt[:, b_, 0:TT]
                own(V.tensor_tensor(x_, score, best.unsqueeze(2).to_broadcast([P, TT, n]), ALU.is_equal))
                own(V.tensor_tensor(x_, x_, kc[:, K_PRIO + NE - n:K_PRIO + NE].unsqueeze(1).to_broadcast([P, TT, n]), ALU.mult))
                own(V.reduce_max(y_, x_, AX.X))
                own(V.tensor_tensor(x_, x_, y_.unsqueeze(2).to_broadcast([P, TT, n]), ALU.is_equal))

            dve.wait_ge(lg_ps, 1)
            own(V.tensor_tensor(lg[:, :, :], pj[:, 0, 0:TT * 36].rearrange("p (t n) -> p t n", n=36), brt[:, :].unsqueeze(1).to_broadcast([P, TT, 36]), ALU.add))
            gl, el = lg[:, :, 0:NG], lg[:, :, NG:36]
            gmax = rt[:, 7, 0:TT]
            own(V.reduce_max(gmax, gl, AX.X))
            V.tensor_tensor(tiles(5, NG), gl, gmax.unsqueeze(2).to_broadcast([P, TT, NG]), ALU.subtract).then_inc(e1_in, 1)
            first_best(gl, gmax, NG, 3, 4)
            own(V.tensor_scalar(tiles(3, NG), tiles(3, NG), -1.0, BIG, ALU.add, ALU.mult))
            own(V.tensor_tensor(el.rearrange("p t (g e) -> p t g e", g=NG), el.rearrange("p t (g e) -> p t g e", g=NG),
                                tiles(3, NG).unsqueeze(3).to_broadcast([P, TT, NG, EG]), ALU.add))
            m1, m2 = rt[:, 7, 8:8 + TT], rt[:, 7, 16:16 + TT]
            own(V.reduce_max(m1, el, AX.X))
            first_best(el, m1, NE, 1, 4)
            own(V.scalar_tensor_tensor(el, tiles(1, NE), -2 * BIG, el, ALU.mult, ALU.add))
            own(V.reduce_max(m2, el, AX.X))
            V.tensor_tensor(rt[:, 6, 0:TT], m2, m1, ALU.subtract).then_inc(e2_in, 1)
            first_best(el, m2, NE, 2, 4)
            V.tensor_tensor(rt[:, 0, :], rt[:, 1, :], rt[:, 2, :], ALU.add).then_inc(hot_in, 1)
            dve.wait_ge(e1_ok, 1)
            gw, ee, dd = rt[:, 7, 24:24 + TT], rt[:, 6, 0:TT], rt[:, 7, 32:32 + TT]
            own(V.reduce_sum(gw, tiles(5, NG), AX.X))
            dve.wait_ge(e2_ok, 1)
            own(V.tensor_scalar(dd, ee, 1.0, None, ALU.add))
            own(V.tensor_tensor(dd, dd, gw, ALU.mult))
            own(V.reciprocal(slotw[:, 0, :], dd))
            V.tensor_tensor(slotw[:, 1, :], slotw[:, 0, :], ee, ALU.mult)
            for t in range(TT):
                V.tensor_scalar(val[:, t, :, 0], rt[:, 2, t * NE:(t + 1) * NE], 0.0, kc[:, K_TOK + t:K_TOK + t + 1], ALU.mult, ALU.add)
                own(V.tensor_scalar(val[:, t, :, 1], rt[:, 2, t * NE:(t + 1) * NE], float(T), kc[:, K_TOK + TT + t:K_TOK + TT + t + 1], ALU.mult, ALU.add))
            dve.wait_ge(pos_ps, 1)
            own(V.scalar_tensor_tensor(pv[:, :, :], pj[:, 1, 0:TT * NE].rearrange("p (t e) -> p t e", e=NE), float(COUNT_SHIFT), tiles(0, NE), ALU.add, ALU.mult))
            own(V.reduce_max(rt[:, 7, 40:41], pj[:, 1, TT * NE:(TT + 1) * NE], AX.X))
            V.tensor_copy(cnt[:, :], rt[0:1, 7, 40:41]).then_inc(cnt_ok, 1)

            dve.sem_inc(hf_ok, 1)
            dve.sem_inc(yo_ok, 1)

            def tail(r, i, t):
                src, s, loads = moe_raw(t)
                dve.wait_ge(wh_ok, r * R_PAIRS + i * 24 + (MIX_PAIRS + t + 1))
                V.tensor_tensor(wl[:, t % RING, :, :], src, wh[:, t % RING, :, :].bitcast(F32), ALU.subtract).then_inc(wl_ok, 1)

            def x_tail(E, par):
                dve.wait_ge(xh_ok, E + 1)
                V.tensor_tensor(xsp[par][:, :, CAP:P], cb[:, 0, :].rearrange("p (k n) -> p k n", k=KD), xsp[par][:, :, 0:CAP].bitcast(F32), ALU.subtract).then_inc(xl_ok, 1)

            def up_copy(E):
                dve.wait_ge(u_f, E + 1)
                V.tensor_copy(us[:, :, :], pj[:, 1, :].rearrange("p (m f) -> p f m", f=KF)).then_inc(us_ok, 1)

            def hidden(E):
                dve.wait_ge(sg_ok, E + 1)
                V.tensor_tensor(sg[:, :], cb[:, 1, 0:KF * CAP], sg[:, :], ALU.mult).then_inc(hq_ok, 1)
                dve.wait_ge(hq_ok, E + 1)
                V.tensor_tensor(hf[:, :], cb[:, 1, KF * CAP:2 * KF * CAP], sg[:, :], ALU.mult).then_inc(hf_ok, 1)

            def hidden_tail(E):
                dve.wait_ge(hh_ok, E + 1)
                V.tensor_tensor(hsp[:, :, CAP:P], hf[:, :].rearrange("p (f n) -> p f n", f=KF), hsp[:, :, 0:CAP].bitcast(F32), ALU.subtract).then_inc(hl_ok, 1)

            def y_sum(E, par):
                dve.wait_ge(yb_ok, E + 1)
                dve.wait_ge(out_ok, E + 1)
                V.tensor_tensor(yo[:, par, :].rearrange("p (a n) -> p a n", a=2), pj[0:CAP, 2:4, :], yb[:, :].rearrange("p (a n) -> p a n", a=2), ALU.add).then_inc(yo_ok, 1)

            def moe_round(r):
                E0, n0 = r * NE, r * (NE // 2)
                if not isinstance(r, int):
                    dve.wait_ge(out_ok, E0 + 2)
                    dve.wait_ge(it_ok, r)
                    V.tensor_scalar(iot[:, :], iot[:, :], float(CAP), None, ALU.add).then_inc(it_ok, 1)
                    dve.wait_ge(it_ok, r + 1)
                else:
                    V.tensor_copy(iot[:, :], kc[:, K_SLOT:K_SLOT + CAP]).then_inc(it_ok, 1)
                    dve.wait_ge(it_ok, 1)
                for t in range(TT):
                    m = V.tensor_tensor(hot[:, t, :, :], pv[:, t, :].unsqueeze(2).to_broadcast([P, NE, CAP]),
                                        iot[:, :].unsqueeze(1).to_broadcast([P, NE, CAP]), ALU.is_equal)
                m.then_inc(hot_ok, 1)
                for t in range(LEAD):
                    tail(r, 0, t)
                dve.wait_ge(tab_ps, r + 1)
                ptab = cb[0:CAP, 2, 0:2 * NE].rearrange("p (e a) -> p e a", a=2)
                V.tensor_scalar(tok_tab[:, :], ptab[:, :, 0], 1024.0, None, ALU.add)
                V.tensor_scalar(dst_tab[:, :], ptab[:, :, 1], 2048.0, None, ALU.add).then_inc(tab_ok, 1)
                x_tail(E0, 0)
                for t in range(8):
                    tail(r, 0, t + LEAD)
                    if t == 4:
                        x_tail(E0 + 1, 1)
                up_copy(E0)

                def expert(i, e, par, t, last):
                    E = E0 + i * 2 + e
                    for s in range(E_PAIRS):
                        tail(r, i, t + s + LEAD)
                        if s == 4:
                            hidden(E - 1)
                        if s == 5:
                            if not last:
                                x_tail(E + 1, 1 - par)
                            hidden_tail(E - 1)
                        if s == 7:
                            up_copy(E)
                    y_sum(E - 1, 1 - par)

                with dve.Fori(0, NE // 2 - 1, 1) as i:
                    expert(i, 1, 1, 8, False)
                    expert(i, 2, 0, 20, False)
                expert(0, NE - 1, 1, 8 + E_PAIRS * (NE - 2), True)
                tail(r, 0, R_PAIRS - 1)
                hidden(E0 + NE - 1)
                hidden_tail(E0 + NE - 1)
                y_sum(E0 + NE - 1, 1)

            moe_round(0)
            most = dve.value_load(cnt[0:1, 0:1], min_val=0, max_val=T)
            with dve.Fori(1, ROUNDS, 1) as r:
                with dve.If(most > r * CAP):
                    moe_round(r)

            dve.wait_ge(wr_in, 32)
            for t in range(TT):
                dve.wait_ge(y_in[t], 32)
                own(V.scalar_tensor_tensor(x2[:, t, :], yin[0][:, t, :], slotw[:, 0, t:t + 1], x2[:, t, :], ALU.mult, ALU.add))
                V.scalar_tensor_tensor(x2[:, t, :], yin[1][:, t, :], slotw[:, 1, t:t + 1], x2[:, t, :], ALU.mult, ALU.add).then_inc(x3_ok, 1)
            dve.wait_ge(sq_ok, 5 * TT)
            rstd(5, ssq[:, 0:TT], TT, D)
            for t in range(TT):
                V.scalar_tensor_tensor(x2[:, t, :], x2[:, t, :], stat[:, 2, t:t + 1], wrow[:, :], ALU.mult, ALU.mult).then_inc(fin_ok, 1)

        @block.gpsimd
        def _(pool):
            pool.memset(onesq[:, :], 1.0).then_inc(zero_ok, 1)
            pool.sem_inc(out_ok, 2)
            pool.wait_ge(hTl_ok, KD)
            pool.memset(wgh[:, :, :].bitcast(F32), 0.0).then_inc(zero_ok, 1)
            pool.memset(convx[:, :, 0:3], 0.0)
            pool.memset(mva[:, :, :, DV:DA], 1.0)
            pool.memset(wgl[:, :, :].bitcast(F32), 0.0).then_inc(zero_ok, 1)
            pool.wait_ge(lg_ps, 1)
            pool.memset(xg[:, :, :], 0.0).then_inc(zero_ok, 1)
            pool.wait_ge(h2_out, 16 * TT)
            pool.wait_ge(zero_ok, 4)

            def gather(E, e, par, n):
                if n is not None:
                    pool.wait_ge(xT_ps, E - 1)
                pool.sem_inc(pool_past, 1)
                pool.tensor_copy(tok_now[:, par:par + 1], tok_tab[:, e:e + 1] if isinstance(e, int) else tok_tab[:, bass.ds(e, 1)]).then_inc(tok_c, 1)
                pool.wait_ge(tok_c, E + 1)
                pool.sem_inc(pool_past, 1)
                pool.indirect_dma_start(xg[:, par, :], None, h_dram, bass.IndirectOffsetOnAxis(ap=tok_now[:, par:par + 1], axis=0),
                                        bounds_check=T - 1, oob_is_err=False).then_inc(gat[par], 16)

            def scatter(E, e, par):
                pool.wait_ge(yo_ok, E + 2)
                pool.sem_inc(pool_past, 1)
                pool.tensor_copy(dst_now[:, par:par + 1], dst_tab[:, e:e + 1] if isinstance(e, int) else dst_tab[:, bass.ds(e, 1)]).then_inc(dst_c, 1)
                pool.wait_ge(dst_c, E + 1)
                pool.sem_inc(pool_past, 1)
                pool.indirect_dma_start(y_dram, bass.IndirectOffsetOnAxis(ap=dst_now[:, par:par + 1], axis=0), yo[:, par, :], None,
                                        bounds_check=2 * T - 1, oob_is_err=False).then_inc(sca, 16)
                pool.wait_ge(sca, E * 16 + 16)
                pool.sem_inc(out_ok, 1)

            def moe_round(r):
                E0 = r * NE
                pool.wait_ge(tab_ok, r + 1)
                gather(E0, 0, 0, None)
                gather(E0 + 1, 1, 1, None)
                with pool.Fori(0, NE // 2 - 1, 1) as i:
                    gather(E0 + i * 2 + 2, i * 2 + 2, 0, 0)
                    scatter(E0 + i * 2, i * 2, 0)
                    gather(E0 + i * 2 + 3, i * 2 + 3, 1, 0)
                    scatter(E0 + i * 2 + 1, i * 2 + 1, 1)
                scatter(E0 + NE - 2, NE - 2, 0)
                scatter(E0 + NE - 1, NE - 1, 1)

            moe_round(0)
            pool.wait_ge(cnt_ok, 1)
            most = pool.value_load(cnt[0:1, 0:1], min_val=0, max_val=T)
            with pool.Fori(1, ROUNDS, 1) as r:
                with pool.If(most > r * CAP):
                    moe_round(r)
            pool.sem_inc(scat_ok, 1)


def constants():
    import numpy as np
    f = np.float32
    k = np.zeros((P, K_END), f)
    m, l = np.arange(P)[:, None], np.arange(P)[None, :]
    k[:, K_IDENT:K_IDENT + P] = m == l
    for h in range(H):
        g = GAMMA[h]
        k[:, K_RMASK + h * P:K_RMASK + (h + 1) * P] = (m <= l) * f(g ** -float(P))
        k[h, K_SELH + h * P:K_SELH + (h + 1) * P] = 1
        k[:, K_QDEC + h * P:K_QDEC + (h + 1) * P] = (g ** (l + 1.0)).astype(f)
        k[:, K_KDEC + h] = (g ** (P - 1.0 - m[:, 0]) * DK ** -0.5).astype(f)
    k[:, K_NOTYET:K_NOTYET + P] = np.where(m > l, f(BIG), f(0))
    k[:, K_BEFORE:K_BEFORE + P] = m < l
    k[:, K_SEL64:K_SEL64 + CAP] = (m % CAP) == l[:, :CAP]
    freq = (f(1.0) / (f(10000.0) ** (np.arange(0, DK, 2, dtype=f) / f(DK)))).astype(f)
    ang = np.arange(T, dtype=f)[:, None] * freq[None, :]
    for t in range(TT):
        k[:, K_COS + 64 * t:K_COS + 64 * (t + 1)] = np.cos(ang[t * P:(t + 1) * P])
        k[:, K_SIN + 64 * t:K_SIN + 64 * (t + 1)] = np.sin(ang[t * P:(t + 1) * P])
        k[:, K_TOK + t] = np.arange(P) + t * P - 1024
        k[:, K_TOK + TT + t] = np.arange(P) + t * P - 2048
    k[:, K_SLOT:K_SLOT + CAP] = np.arange(CAP) + COUNT_SHIFT
    k[:, K_PRIO:K_PRIO + NE] = NE - np.arange(NE)
    return k


_INS = ['x', 'norm_mix_w', 'w_in', 'ret_gn_w', 'w_ret_branch', 'mlstm_conv_w', 'mlstm_conv_b', 'b_igate', 'b_fgate',
        'mlstm_gn_w', 'w_mlstm_branch', 'w_out', 'norm_ffn_w', 'w_group', 'b_group', 'w_expert_router',
        'b_expert_router', 'w_gate', 'w_up', 'w_down', 'norm_final_w']


def kernel(**inputs):
    import numpy as _np
    import concourse.bacc as _bacc
    from concourse import mybir as _mybir
    from concourse.bass_utils import run_bass_kernel_spmd as _run

    nc = _bacc.Bacc("TRN2", target_bir_lowering=False, num_devices=1)
    arrays, args = {}, []
    for name in _INS:
        a = _np.ascontiguousarray(inputs[name])
        arrays[f"in_{name}_dram"] = a
        args.append(nc.dram_tensor(f"in_{name}_dram", a.shape, _mybir.dt.from_np(a.dtype), kind="ExternalInput").ap())
    arrays["in_consts_dram"] = constants()
    args.append(nc.dram_tensor("in_consts_dram", arrays["in_consts_dram"].shape, F32, kind="ExternalInput").ap())
    args.append(nc.dram_tensor("out_0_dram", (1, T, D), F32, kind="ExternalOutput").ap())
    hybrid_block(nc, *args)
    r = _run(nc, [arrays], core_ids=[0])
    return r.results[0]["out_0_dram"]
```

```python
import concourse.bass as bass
from concourse import mybir
from contextlib import ExitStack

F32 = mybir.dt.float32
F32R = mybir.dt.float32r
F16 = mybir.dt.float16
I32 = mybir.dt.int32
ALU = mybir.AluOpType
ACT = mybir.ActivationFunctionType
AX = mybir.AxisListType

P = 128
T = 512
D = 1024
TT = T // P
KD = D // P
H = 4
DK = 128
DV = 256
DA = DV + 1
NE, NG, EG = 32, 4, 8
FE = 512
KF = FE // P
CAP = 64
ROUNDS = T // CAP
EPS = 1e-6
BIG = 1e30
NO_TOKEN = 1024
KB = 1024

C_RQ, C_RK, C_RV, C_RG = 0, 512, 1024, 2048
C_MQ, C_MK, C_MV, C_MO = 3072, 3584, 4096, 5120
C_IF, C_GR, C_GM = 6144, 6152, 7176
B_RQ, B_RK, B_RV, B_MQ, B_MK, B_MV, B_RG, B_GR, B_GM, B_MO, B_WR, B_WM, B_WO = 0, 1, 2, 4, 5, 6, 8, 10, 12, 14, 16, 18, 20
BLOCKS = 22
IN_COLS = [C_RQ, C_RK, C_RV, C_RV + 512, C_MQ, C_MK, C_MV, C_MV + 512, C_RG, C_RG + 512,
           C_GR, C_GR + 512, C_GM, C_GM + 512, C_MO, C_MO + 512]
CHANNEL_MAJOR = {B_MQ, B_MK, B_GR, B_GR + 1, B_GM, B_GM + 1, B_WR, B_WR + 1, B_WM, B_WM + 1}
MIX_PAIRS = 4 * BLOCKS
RING = 4
LEAD = RING - 1
MOE_RING = 6
MOE_LEAD = MOE_RING - 1
RSTD_STEPS = 5
MIX_RAW = 3
MOE_RAW = 12
IN_FLIGHT = 4
E_PAIRS = 12
R_PAIRS = NE * E_PAIRS
POOL_PAIR = 10

K_IDENT = 0
K_RMASK = K_IDENT + P
K_NOTYET = K_RMASK + H * P
K_BEFORE = K_NOTYET + P
K_QDEC = K_BEFORE + P
K_SEL64 = K_QDEC + H * P
K_COS = K_SEL64 + CAP
K_SIN = K_COS + TT * 64
K_KDEC = K_SIN + TT * 64
K_SLOT = K_KDEC + H
K_PRIO = K_SLOT + CAP
K_TOK = K_PRIO + NE
K_SELH = K_TOK + TT
K_END = K_SELH + H * P

GAMMA = [1.0 - 2.0 ** (-5.0 - h) for h in range(H)]


def hybrid_block(nc, x, norm_mix_w, w_in, ret_gn_w, w_ret, conv_w, conv_b, b_i, b_f, mlstm_gn_w, w_mlstm, w_out,
                 norm_ffn_w, w_group, b_group, w_router, b_router, w_gate, w_up, w_down, norm_final_w, consts, out):
    ctx = ExitStack()
    with ctx:
        base = -(-nc.sbuf_base // 64) * 64

        def at(name, kib, shape, dt=F32):
            return nc.alloc_sbuf_tensor_at(name, shape, dt, offset=base + int(kib * KB))

        def sem(name):
            return ctx.enter_context(nc.semaphore(name))

        hTh = at("hTh", 0, [P, KD, T], F32R)
        hTl = at("hTl", 16, [P, KD, T], F32R)
        mixTh = at("mixTh", 0, [P, KD, T], F32R)
        mixTl = at("mixTl", 16, [P, KD, T], F32R)
        rqn = at("rqn", 32, [P, TT, 512])
        rqT = at("rqT", 40, [P, H, T])
        rkT = at("rkT", 48, [P, H, T])
        rkn = at("rkn", 56, [P, TT, 512])
        dT = at("dT", 32, [P, H, T])
        Cst = at("Cst", 40, [P, H, DA])
        retTh = at("retTh", 32, [P, KD, T], F32R)
        retTl = at("retTl", 48, [P, KD, T], F32R)
        mrgTh = at("mrgTh", 32, [P, KD, T], F32R)
        mrgTl = at("mrgTl", 48, [P, KD, T], F32R)
        rvo = at("rvo", 64, [P, TT, D])
        msg = at("msg", 64, [P, 2, 512])
        convx = at("convx", 80, [P, 4, 3 + T])
        rtmp = at("rtmp", 88.25, [P, 2, 512])
        Rst = at("Rst", 88.25, [P, H, DV])
        csg = at("csg", 92.25, [P, T])
        selh = at("selh", 92.25, [H, H * P])
        rsg = at("rsg", 80, [P, 4, 512])
        mrg = at("mrg", 80, [P, KD, T])
        raw_moe = [at(f"raw_moe{s}", k, [P, 4, 512]) for s, k in
                   enumerate([64, 72, 0, 8, 16, 24, 80, 88, 32, 40, 48, 56])]
        wh = at("wh", 96, [P, RING, 2, 512], F32R)
        wl = at("wl", 112, [P, RING, 2, 512], F32R)
        wh_more = at("wh_more", 128, [P, MOE_RING - RING, 2, 512], F32R)
        wl_more = at("wl_more", 136, [P, MOE_RING - RING, 2, 512], F32R)
        xt = at("xt", 128, [P, TT, D])
        mva = at("mva", 128, [P, TT, H, DA])
        x2 = at("x2", 128, [P, TT, D])
        raw_mix = [at(f"raw_mix{s}", 144.5 + 8 * s, [P, 4, 512]) for s in range(MIX_RAW)]
        h2T = at("h2T", 144.5, [P, KD, T])
        at_slot = at("at_slot", 144.5, [P, 2, TT, CAP])
        yo = at("yo", 144.5, [CAP, 2, D])
        yb = at("yb", 152.5, [CAP, D])
        gs = at("gs", 156.5, [P, 2, KF, P])
        xg = at("xg", 160.5, [CAP, 2, D])
        xs0 = at("xs0", 168.5, [P, TT, D])
        wgh = at("wgh", 168.5, [P, KD, P], F32R)
        wgl = at("wgl", 172.5, [P, KD, P], F32R)
        grow = at("grow", 174.5, [H, 5, T])
        gbc = at("gbc", 184.5, [P, H, T])
        mqT = at("mqT", 168.5, [P, H, T])
        mkT = at("mkT", 176.5, [P, H, T])
        sgm = at("sgm", 168.5, [P, KD, T])
        h2 = at("h2", 168.5, [P, TT, D])
        xsp = [at(f"xsp{i}", 168.5 + 4 * i, [P, KD, P], F32R) for i in range(2)]
        hsp = at("hsp", 176.5, [P, KF, P], F32R)
        us = at("us", 178.5, [P, KF, P])
        sg = at("sg", 180.5, [P, KF * CAP])
        hf = at("hf", 181.5, [P, KF * CAP])
        wrow = at("wrow", 184.5, [P, D])
        wrt = at("wrt", 188.5, [P, KD, 36])
        brt = at("brt", 189.75, [P, 36])
        rt = at("rt", 190, [P, 8, TT * NE])
        kc = at("kc", 194, [P, K_SELH])
        rest = 194 + (K_SELH * 4 + 63) // 64 * 64 / KB

        class Small:
            top = rest

        def small(name, shape, dt=F32):
            n = 1
            for s in shape[1:]:
                n *= s
            t = at(name, Small.top, shape, dt)
            Small.top += -(-n * 4 // 32) * 32 / KB
            return t

        vrow = at("vrow", 188.5, [64, P])
        wgr = at("wgr", 189, [P, KD, 2 * H])
        vcol = small("vcol", [P, 64])
        bif = small("bif", [H, 2])
        stat = small("stat", [P, 4, 16])
        rret = small("rret", [P, 16])
        ssq = small("ssq", [P, 16])
        mprev = small("mprev", [H, TT + 1])
        gcol = small("gcol", [P, 5, 16])
        gex = small("gex", [P, 3, 16])
        rden = small("rden", [P, 2])
        st = small("st", [P, 2, P])
        over = Small.top - 2 * P * 4 / KB
        wk = small("wk", [P, 2, P])
        what = at("what", over, [P, 2, TT, NE])
        lg = at("lg", over + 1, [P, TT, 36])
        iot = at("iot", over + 1.625, [P, CAP])
        slotw = small("slotw", [P, 2, TT])
        cnt = small("cnt", [1, 1], I32)
        tok_tab = small("tok_tab", [CAP, NE], I32)
        w_tab = small("w_tab", [CAP, NE])
        w_now = small("w_now", [CAP, 2])
        tok_out = small("tok_out", [CAP, 1], I32)
        nwc = small("nwc", [P, KD])
        pos = small("pos", [P, 2, TT])
        tok_now = small("tok_now", [CAP, 2], I32)
        onesq = small("onesq", [P, P])
        ones16 = at("ones16", Small.top, [P, P], F16)
        before16 = at("before16", Small.top + 0.25, [P, P], F16)
        hot16 = at("hot16", Small.top + 0.5, [P, TT * NE], F16)
        rsq = small("rsq", [P, DV])
        assert base + Small.top * KB <= nc.sbuf_usable_end, (base + Small.top * KB, nc.sbuf_usable_end)

        pj = ctx.enter_context(nc.psum_tensor("pj", [P, 4, 512], F32))
        cb = ctx.enter_context(nc.psum_tensor("cb", [P, 4, 512], F32))

        h_dram = nc.dram_tensor("h_scratch", [T, D], F32).ap()
        x_dram = nc.dram_tensor("x_scratch", [T, D], F32).ap()

        c_in, v_in, wg_in, br_in, wr_in, xr_in = (sem(n) for n in (
            "consts_in", "vectors_in", "gate_w_in", "router_in", "norm_row_in", "x_again_in"))
        x_in = [sem(f"x_in{t}") for t in range(TT)]
        raw_in = [sem(f"raw_in{s}") for s in range(MIX_RAW)]
        moe_in = [sem(f"moe_in{s}") for s in range(MOE_RAW)]
        wh_ok, wl_ok = sem("heads_ready"), sem("tails_ready")
        pair_used = sem("pairs_used")
        full = [sem(f"bank_full{i}") for i in range(4)]
        free = [sem(f"bank_free{i}") for i in range(4)]
        v_own, a_own, p_own = sem("vector_own"), sem("scalar_own"), sem("pool_own")
        sq_ok, var_ok, root_ok = sem("squares"), sem("variance"), sem("root")
        vT, vC, zero_ok = sem("vectors_turned"), sem("vector_columns"), sem("memsets")
        xs_ok = [sem("x_scaled_even"), sem("x_scaled_odd")]
        it_ok, r_done, pool_tail, st_in, wrt_ok = sem("slot_numbers_ready"), sem("round_out"), sem("pool_tails"), sem("stream_in_dram"), sem("router_weights_ready")
        hT_ps, hTh_ok, hTl_ok = sem("h_turned"), sem("h_heads"), sem("h_tails")
        gwh_ok, gwl_ok, g_ps, grow_a = sem("gate_w_heads"), sem("gate_w_tails"), sem("gates_in_psum"), sem("gate_rows_copied")
        f_abs, f_log, grow_ok, gtiny, gcol_ok = (sem(n) for n in (
            "forget_abs", "forget_log", "gate_rows_ready", "gate_columns_in_psum", "gate_columns_ready"))
        gex_in, gex_ok = sem("gate_exponents"), sem("gate_exps")
        gb_ps, gb_ok, dt_in, dt_ok, wint_ok = (sem(n) for n in (
            "G_broadcast", "G_copied", "decay_exponents", "decay_ready", "inter_weight_ready"))
        rope_ok, rqT_ps, rqT_ok, rkT_ps, rkT_ok = (sem(n) for n in (
            "rotated", "rq_turned", "rqT_ready", "rk_turned", "rkT_ready"))
        r_s, r_st, r_o, r_out, r_R = (sem(n) for n in ("ret_scores", "ret_masked", "ret_products", "ret_out", "ret_state"))
        conv_a, conv_v, conv_s, mqk_ok, wq_ok = (sem(n) for n in (
            "conv_first_tap", "conv_taps", "conv_sigmoid", "mqk_ready", "weighted_q_ready"))
        m_s, m_st, m_wk, m_o, m_rc, m_C, m_h = (sem(n) for n in (
            "ml_scores", "ml_weighted", "ml_keys", "ml_products", "ml_denominator", "ml_state", "ml_out"))
        rg_s, ret_ok, mo_v, hm_ok = sem("rgate_sigmoid"), sem("ret_gated"), sem("ml_gated"), sem("ml_normed")
        tr_ps, tr_h, tr_l = sem("out_turned"), sem("out_heads"), sem("out_tails")
        mg_ok, mgh_ok, mgl_ok = sem("merged"), sem("merged_heads"), sem("merged_tails")
        h2_ok, h2_out, h2T_ps, h2T_v, h2T_a = (sem(n) for n in (
            "h2_ready", "h2_in_dram", "h2_turned", "h2T_by_vector", "h2T_by_scalar"))
        lg_ps, e1_in, e1_ok, e2_in, e2_ok, hot_in, pos_ps, hot_ok, tab_ps, tab_ok, cnt_ok = (sem(n) for n in (
            "logits", "group_exponents", "group_exps", "expert_exponents", "expert_exps", "routed", "positions",
            "one_hot_ready", "table_in_psum", "table_ready", "counts_ready"))
        gat, sca, out_ok = [sem("gathered0"), sem("gathered1")], sem("scattered"), sem("outputs_out")
        tok_c, w_c, ww_ok, wt_ps, wt_ok, yw_ok = (sem(n) for n in (
            "token_column", "weight_column", "weights_by_expert", "weights_in_psum", "weight_table_ready", "y_weighted"))
        xT_ps, xh_ok, xl_ok = sem("expert_x_turned"), sem("expert_x_heads"), sem("expert_x_tails")
        g_f, u_f, gs_ok, us_ok, gt_ps, sg_ok, hq_ok, hf_ok, hh_ok, hl_ok, y_f, yb_ok, yo_ok = (sem(n) for n in (
            "gate_full", "up_full", "gate_copied", "up_copied", "gate_up_turned", "gate_sigmoid", "silu_ready", "hidden_ready",
            "hidden_heads", "hidden_tails", "y_full", "y_tails_copied", "y_ready"))
        x3_in = [sem(f"x3_in{t}") for t in range(TT)]
        scat_ok, fin_ok, out_in = sem("all_scattered"), sem("out_ready"), sem("out_stored")
        pe_past, pool_past, sp_past = sem("tensor_past_waits"), sem("pool_past_waits"), sem("sync_past_waits")
        block = ctx.enter_context(nc.Block())

        def stage_of(st):
            if st < 2:
                return st, 0
            if st == R_PAIRS // 4 - 1:
                return 2, NE - 1
            kind = (st - 2) % 3
            return kind, 1 + (st - 2) // 3 - (kind == 2)

        def wait_pair_used(eng, r, i, t):
            used0 = 3 * BLOCKS + r * (3 * R_PAIRS // 4)
            if t < MOE_RING and isinstance(r, int):
                if t < 3:
                    eng.wait_ge(pair_used, used0 - 3 + t + 1)
                elif t == 3:
                    eng.wait_ge(full[3], BLOCKS)
                else:
                    eng.wait_ge(st_in, 16 * TT)
                return
            if t < MOE_RING:
                r, t, used0 = r - 1, t + R_PAIRS, used0 - 3 * R_PAIRS // 4
            st, j = divmod(t - MOE_RING, 4)
            if j < 3:
                eng.wait_ge(pair_used, used0 + 3 * st + j + 1 + i * 18)
            else:
                kind, e = stage_of(st)
                eng.wait_ge((g_f, u_f, y_f)[kind], r * NE + i * 2 + e + 1)

        def wait_mix_pair(eng, q):
            if q % 4 == 3:
                eng.wait_ge(full[3], q // 4 + 1)
            else:
                eng.wait_ge(pair_used, 3 * (q // 4) + q % 4 + 1)

        def moe_raw(t):
            m = t // 2
            return raw_moe[m % MOE_RAW][:, 2 * (t % 2):2 * (t % 2) + 2, :], m % MOE_RAW, m // MOE_RAW + 1

        def moe_split(w, more, t):
            s = t % MOE_RING
            return w[:, s, :, :] if s < RING else more[:, s - RING, :, :]

        def pools(t):
            return (t + E_PAIRS - POOL_PAIR) // E_PAIRS

        def wait_tail(eng, r, i, t):
            if t % E_PAIRS == POOL_PAIR:
                eng.wait_ge(pool_tail, r * NE + i * 2 + pools(t))
            else:
                eng.wait_ge(wl_ok, r * (R_PAIRS - NE) + i * 22 + (MIX_PAIRS + t + 1 - pools(t)))

        LOADS = R_PAIRS // 2 // MOE_RAW

        @block.sync
        def _(sp):
            for t in range(TT):
                sp.dma_start(xt[:, t, :], x[0][t * P:(t + 1) * P, :]).then_inc(x_in[t], 16)
            sp.dma_start(kc[:, :], consts[:, 0:K_SELH]).then_inc(c_in, 16)
            sp.dma_start(selh[:, :], consts[0:H, K_SELH:K_END]).then_inc(c_in, 16)
            sp.dma_start(vrow[0:8, :], norm_mix_w.rearrange("l (k p) -> (l k) p", p=P)).then_inc(v_in, 16)
            sp.dma_start(vrow[8:16, :], ret_gn_w.rearrange("l (k p) -> (l k) p", p=P)).then_inc(v_in, 16)
            sp.dma_start(vrow[16:24, :], mlstm_gn_w.rearrange("l (k p) -> (l k) p", p=P)).then_inc(v_in, 16)
            sp.dma_start(vrow[24:32, :], conv_b.rearrange("l (k p) -> (l k) p", p=P)).then_inc(v_in, 16)
            sp.dma_start(vrow[32:64, :], conv_w.rearrange("l w o (k p) -> (l w o k) p", p=P)).then_inc(v_in, 16)

            def mix_chunk(n):
                b, half = divmod(n, 2)
                if b < B_WR:
                    w, c0 = w_in[0], IN_COLS[b]
                else:
                    w, c0 = (w_ret, w_mlstm, w_out)[(b - B_WR) // 2][0], 512 * (b % 2)
                if n >= MIX_RAW:
                    sp.wait_ge(wl_ok, 2 * (n - MIX_RAW) + 2)
                sp.dma_start(raw_mix[n % MIX_RAW][:, :, :],
                             w[512 * half:512 * (half + 1), c0:c0 + 512].rearrange("(k p) n -> p k n", p=P))\
                    .then_inc(raw_in[n % MIX_RAW], 16)

            for n in range(MIX_RAW):
                mix_chunk(n)
            sp.wait_ge(vT, 1)
            sp.dma_start(wgr[:, :, :], w_in[0][:, C_IF:C_IF + 2 * H].rearrange("(k p) n -> p k n", p=P)).then_inc(wg_in, 16)
            sp.dma_start(bif[:, 0:1], b_i.rearrange("l h -> h l")).then_inc(wg_in, 16)
            sp.dma_start(bif[:, 1:2], b_f.rearrange("l h -> h l")).then_inc(wg_in, 16)
            for n in range(MIX_RAW, 2 * BLOCKS):
                if n == 2 * B_WM + 2:
                    sp.wait_ge(tr_ps, 2 * KD)
                    sp.dma_start(x2[:, :, :], x[0].rearrange("(t p) d -> p t d", p=P)).then_inc(xr_in, 16)
                    sp.dma_start(wrow[:, :], norm_ffn_w[0:1, :].to_broadcast([P, D])).then_inc(wr_in, 16)
                    sp.dma_start(wrt[:, :, 0:NG], w_group[0].rearrange("(p k) n -> p k n", k=KD)).then_inc(br_in, 16)
                    sp.dma_start(wrt[:, :, NG:36], w_router[0].rearrange("(p k) n -> p k n", k=KD)).then_inc(br_in, 16)
                    sp.dma_start(nwc[:, :], norm_ffn_w[0].rearrange("(p k) -> p k", k=KD)).then_inc(br_in, 16)
                    sp.dma_start(brt[:, 0:NG], b_group[0:1, :].to_broadcast([P, NG])).then_inc(br_in, 16)
                    sp.dma_start(brt[:, NG:36], b_router[0:1, :].to_broadcast([P, NE])).then_inc(br_in, 16)
                mix_chunk(n)

            def moe_chunk(m, r, i, used):
                kind, e = stage_of(m // 2)
                e, half, s = i * 2 + e, m % 2, m % MOE_RAW
                if used:
                    n = m - IN_FLIGHT
                    sp.wait_ge(moe_in[n % MOE_RAW], r * (16 * LOADS) + i * 16 + 16 * (n // MOE_RAW + 1))
                    sp.sem_inc(sp_past, 1)
                    if 2 * (m - MOE_RAW) % E_PAIRS == POOL_PAIR:
                        wait_tail(sp, r, i, 2 * (m - MOE_RAW))
                        sp.sem_inc(sp_past, 1)
                    wait_tail(sp, r, i, 2 * (m - MOE_RAW) + 1)
                if kind == 2:
                    wd = w_down[0][e] if isinstance(e, int) else w_down[0][bass.ds(e, 1)].rearrange("a f d -> (a f) d")
                    sp.dma_start(raw_moe[s][:, :, :].rearrange("p (f c) n -> p f (c n)", f=2),
                                 wd.rearrange("(p f) n -> p f n", f=KF)[:, 2 * half:2 * half + 2, :]).then_inc(moe_in[s], 16)
                else:
                    w = (w_gate, w_up)[kind][0]
                    wg = w[e] if isinstance(e, int) else w[bass.ds(e, 1)].rearrange("a f d -> (a f) d")
                    sp.dma_start(raw_moe[s][:, :, :],
                                 wg.rearrange("(p k) n -> p k n", k=KD)[:, 4 * half:4 * half + 4, :]).then_inc(moe_in[s], 16)

            def round_chunks(r):
                last = R_PAIRS // 2 - MOE_RAW

                if not isinstance(r, int):
                    for m in range(MOE_RAW):
                        moe_chunk(m, r, 0, True)
                with sp.Fori(0, last // MOE_RAW - 1, 1) as i:
                    for m in range(MOE_RAW, 2 * MOE_RAW):
                        moe_chunk(m, r, i, True)
                for m in range(last, last + MOE_RAW):
                    moe_chunk(m, r, 0, True)

            sp.wait_ge(mo_v, 8)
            moe_chunk(0, 0, 0, False)
            moe_chunk(1, 0, 0, False)
            sp.wait_ge(full[3], B_WO)
            for m in range(2, 6):
                moe_chunk(m, 0, 0, False)
            sp.wait_ge(mgl_ok, KD)
            moe_chunk(6, 0, 0, False)
            moe_chunk(7, 0, 0, False)
            for t in range(TT):
                sp.wait_ge(free[t], BLOCKS)
                sp.dma_start(x_dram[t * P:(t + 1) * P, :], x2[:, t, :]).then_inc(st_in, 16)
            sp.wait_ge(full[3], BLOCKS)
            moe_chunk(8, 0, 0, False)
            sp.wait_ge(h2_ok, TT)
            for m in range(9, MOE_RAW):
                moe_chunk(m, 0, 0, False)
            round_chunks(0)
            sp.wait_ge(cnt_ok, 1)
            most = sp.value_load(cnt[0:1, 0:1], min_val=0, max_val=T)
            with sp.Fori(1, ROUNDS, 1) as r:
                with sp.If(most > r * CAP):
                    round_chunks(r)

            sp.dma_start(wrow[:, :], norm_final_w.rearrange("(a d) -> a d", a=1).to_broadcast([P, D])).then_inc(wr_in, 16)
            sp.wait_ge(scat_ok, 1)
            for t in range(TT):
                sp.dma_start(x2[:, t, :], x_dram[t * P:(t + 1) * P, :]).then_inc(x3_in[t], 16)
            for t in range(TT):
                sp.wait_ge(fin_ok, t + 1)
                sp.dma_start(out[0][t * P:(t + 1) * P, :], x2[:, t, :]).then_inc(out_in, 16)
            sp.wait_ge(out_in, 16 * TT)

        @block.tensor
        def _(pe):
            def turn(o, i, k=P):
                return nc.tensor.transpose(o, i, kc[0:k, K_IDENT:K_IDENT + k])

            pe.wait_ge(c_in, 32)
            pe.wait_ge(v_in, 80)
            turn(cb[:, 3, 0:64], vrow[:, :], 64).then_inc(vT, 1)
            for t in range(TT):
                pe.wait_ge(xs_ok[t % 2], t // 2 + 1)
                if t == 0:
                    pe.wait_ge(vC, 1)
                for k in range(KD):
                    m = turn((pj, cb)[k // 4][:, k % 4, t * P:(t + 1) * P], xs0[:, t, k * P:(k + 1) * P])
                    if t == TT - 1:
                        m.then_inc(hT_ps, 1)

            def mix_half(b, j, half, ah, al):
                s = j % RING
                if half == 0:
                    pe.wait_ge(wl_ok, 4 * b + j + 1)
                    if b == 0:
                        pe.wait_ge(hTl_ok, max(2 * j + 2, 4))
                for i in (2 * half, 2 * half + 1):
                    if j == 0 and b > 0:
                        pe.wait_ge(free[i], b)
                    cols = slice(i * P, (i + 1) * P)
                    for kk in range(2):
                        k = 2 * j + kk
                        if b in CHANNEL_MAJOR:
                            ops = ((wh[:, s, kk, cols], ah[:, k, :]), (wh[:, s, kk, cols], al[:, k, :]), (wl[:, s, kk, cols], ah[:, k, :]))
                        else:
                            ops = ((ah[:, k, cols], wh[:, s, kk, :]), (al[:, k, cols], wh[:, s, kk, :]), (ah[:, k, cols], wl[:, s, kk, :]))
                        for n, (lhsT, rhs) in enumerate(ops):
                            m = nc.tensor.matmul(pj[:, i, :], lhsT, rhs, start=k == 0 and n == 0, stop=k == KD - 1 and n == 2)
                    if j == 3:
                        m.then_inc(full[i], 1)
                    elif i == 3:
                        m.then_inc(pair_used, 1)

            def ret_scores(c, h):
                i, cs = 4 * c + h, slice(c * P, (c + 1) * P)
                if i == 0:
                    pe.wait_ge(rqT_ok, TT)
                    pe.wait_ge(rkT_ok, TT)
                    pe.wait_ge(gb_ok, H)
                elif i >= 2:
                    pe.wait_ge(r_out, i - 1)
                nc.tensor.matmul(cb[:, i % 2, 0:P], rkT[:, h, cs], rqT[:, h, cs], start=True, stop=True).then_inc(r_s, 1)

            def ret_products(c, h):
                i, cs, hv = 4 * c + h, slice(c * P, (c + 1) * P), slice(h * DV, (h + 1) * DV)
                pe.wait_ge(r_st, i + 1)
                m = nc.tensor.matmul(cb[:, i % 2, P:P + DV], st[:, i % 2, :], rvo[:, c, hv], start=True, stop=c == 0)
                if c > 0:
                    pe.wait_ge(r_R, i - 3)
                    m = nc.tensor.matmul(cb[:, i % 2, P:P + DV], rqT[:, h, cs], Rst[:, h, :], start=False, stop=True)
                if c < TT - 1:
                    if i >= 2:
                        pe.wait_ge(r_R, i - 1)
                    m = nc.tensor.matmul(cb[:, 2 + i % 2, 0:DV], rkn[:, c, h * P:(h + 1) * P], rvo[:, c, hv], start=True, stop=True)
                m.then_inc(r_o, 1)

            def ml_scores(c, h):
                i, cs = 4 * c + h, slice(c * P, (c + 1) * P)
                if i == 0:
                    pe.wait_ge(r_out, 16)
                    pe.wait_ge(r_R, 12)
                    pe.wait_ge(mqk_ok, 8)
                elif i >= 2:
                    pe.wait_ge(m_h, i - 1)
                    pe.wait_ge(m_C, min(i - 1, 12))
                nc.tensor.matmul(cb[:, i % 2, 0:P], mkT[:, h, cs], mqT[:, h, cs], start=True, stop=True)
                turn(cb[:, 2 + i % 2, 0:P], mkT[:, h, cs]).then_inc(m_s, 1)

            def ml_products(c, h):
                i, cs = 4 * c + h, slice(c * P, (c + 1) * P)
                pe.wait_ge(m_st, i + 1)
                m = nc.tensor.matmul(cb[:, i % 2, P:P + DA], st[:, i % 2, :], mva[:, c, h, :], start=True, stop=c == 0)
                if c > 0:
                    pe.wait_ge(m_C, i - 3)
                    pe.wait_ge(wq_ok, H)
                    m = nc.tensor.matmul(cb[:, i % 2, P:P + DA], gbc[:, h, cs], Cst[:, h, :], start=False, stop=True)
                pe.wait_ge(m_wk, i + 1)
                if c < TT - 1:
                    m = nc.tensor.matmul(cb[:, 2 + i % 2, P:P + DA], wk[:, i % 2, :], mva[:, c, h, :], start=True, stop=True)
                m.then_inc(m_o, 1)

            def turn_out(n, src):
                if n == 0:
                    pe.wait_ge(m_h, 16)
                    pe.wait_ge(ret_ok, 16)
                elif n >= 4:
                    pe.wait_ge(tr_l, n - 3)
                if n in (8, 12):
                    pe.wait_ge(hm_ok, (n - 4) // 4)
                for t in range(TT):
                    m = turn(cb[:, n % 4, t * P:(t + 1) * P], src(t, n % KD))
                m.then_inc(tr_ps, 1)

            for b in range(BLOCKS):
                act = (hTh, hTl) if b < B_WR else (retTh, retTl) if b < B_WM else (mixTh, mixTl) if b < B_WO else (mrgTh, mrgTl)
                if b == B_RK:
                    pe.wait_ge(gwl_ok, 2)
                    for k in range(KD):
                        for n, (w_, a_) in enumerate(((wgh, hTh), (wgh, hTl), (wgl, hTh))):
                            m = nc.tensor.matmul(cb[:, 3, :], w_[:, k, :], a_[:, k, :], start=k == 0 and n == 0, stop=k == KD - 1 and n == 2)
                    m.then_inc(g_ps, 1)
                if b == B_RV + 1:
                    pe.wait_ge(grow_ok, 1)
                    pe.wait_ge(rqT_ok, TT)
                    for a in range(3):
                        for c in range(TT):
                            turn(cb[:, 3, a * 16 + c * 4:a * 16 + c * 4 + 4], grow[:, (3, 2, 4)[a], c * P:(c + 1) * P], H)
                    for h in range(H):
                        sel = selh[:, h * P:(h + 1) * P]
                        nc.tensor.matmul(cb[:, 3, 48 + 4 * h:52 + 4 * h], sel, mprev[:, 0:TT], start=True, stop=True)
                        m = nc.tensor.matmul(cb[:, 3, 64 + 4 * h:68 + 4 * h], sel, grow[:, 4, P - 1:T:P], start=True, stop=True)
                    m.then_inc(gtiny, 1)
                if b == B_WR:
                    pe.wait_ge(tr_l, KD)
                if b == B_WM:
                    pe.wait_ge(tr_l, 2 * KD)
                for j in range(4):
                    if b == B_WO:
                        pe.wait_ge(mgl_ok, 2 * j + 2)
                    mix_half(b, j, 0, *act)
                    if B_MQ <= b < B_RG:
                        ret_scores(b - B_MQ, j)
                    if B_RG <= b < B_GM:
                        ml_scores(b - B_RG, j)
                    if b in (B_GM, B_GM + 1):
                        turn_out(4 * (b - B_GM) + j, lambda t, n: rvo[:, t, n * P:(n + 1) * P])
                    if b in (B_WR, B_WR + 1):
                        turn_out(8 + 4 * (b - B_WR) + j, lambda t, n: mva[:, t, n // 2, (n % 2) * P:(n % 2 + 1) * P])
                    mix_half(b, j, 1, *act)
                    if b == B_RV:
                        pe.wait_ge(rope_ok, j + 1)
                        if j == 3:
                            pe.wait_ge(grow_a, 2)
                        for h in range(H):
                            m = turn(cb[:, j, h * P:(h + 1) * P], rqn[:, j, h * P:(h + 1) * P])
                        m.then_inc(rqT_ps, 1)
                    if b == B_RV + 1:
                        pe.wait_ge(rope_ok, TT + j + 1)
                        if j == 3:
                            pe.wait_ge(gcol_ok, 1)
                        for h in range(H):
                            m = turn(cb[:, j, h * P:(h + 1) * P], rkn[:, j, h * P:(h + 1) * P])
                        m.then_inc(rkT_ps, 1)
                        for h in ((), (0,), (1,), (2, 3))[j]:
                            pe.wait_ge(rkT_ok, h + 1)
                            nc.tensor.matmul(cb[:, h, :], selh[:, h * P:(h + 1) * P], grow[:, 4, :],
                                             start=True, stop=True).then_inc(gb_ps, 1)
                    if B_MQ <= b < B_RG:
                        ret_products(b - B_MQ, j)
                    if B_RG <= b < B_GM:
                        ml_products(b - B_RG, j)

            def turn_stream(t):
                pe.wait_ge(free[t], BLOCKS)
                for half in range(2):
                    bank = cb[:, 2 * t + half, :] if t < 2 else pj[:, 2 * t + half - TT, :]
                    for k in range(4):
                        m = turn(bank[:, k * P:(k + 1) * P], x2[:, t, 4 * half + k:D:KD])
                    m.then_inc(h2T_ps, 1)

            def logits(t):
                pe.wait_ge(h2T_v, t + 1)
                pe.wait_ge(h2T_a, t + 1)
                for k in range(KD):
                    m = nc.tensor.matmul(cb[:, 0, t * 36:(t + 1) * 36], h2T[:, k, t * P:(t + 1) * P], wrt[:, k, :], start=k == 0, stop=k == KD - 1)
                return m

            pe.wait_ge(tr_l, 2 * KD)
            for t in range(3):
                turn_stream(t)
            pe.wait_ge(wrt_ok, 1)
            logits(0)
            turn_stream(3)
            for t in range(1, TT):
                m = logits(t)
            m.then_inc(lg_ps, 1)
            pe.wait_ge(hot_in, 1)
            for t in range(TT + 1):
                for t2 in range(min(t + 1, TT)):
                    m = nc.tensor.matmul(cb[:, 1, t * NE:(t + 1) * NE], (before16 if t2 == t else ones16)[:, :], hot16[:, t2 * NE:(t2 + 1) * NE],
                                         start=t2 == 0, stop=t2 == min(t, TT - 1))
            m.then_inc(pos_ps, 1)

            def weights_pair(r, i, t, lhs, banks, first, last):
                wait_tail(pe, r, i, t)
                one = banks[0] == banks[1]
                for kk in range(2):
                    for n, w_ in enumerate((moe_split(wh, wh_more, t), moe_split(wl, wl_more, t))):
                        m = nc.tensor.matmul(pj[:, banks[kk], :], lhs(kk), w_[:, kk, :],
                                             start=first and n == 0 and not (one and kk == 1),
                                             stop=last and n == 1 and not (one and kk == 0))
                return m

            def turn_x(E, par, n):
                if E is not None:
                    pe.wait_ge(xl_ok, E)
                pe.wait_ge(gat[par], n * 16 + 16)
                pe.sem_inc(pe_past, 1)
                for k in range(KD):
                    m = turn(cb[:, 0, k * CAP:(k + 1) * CAP], xg[:, par, k * P:(k + 1) * P], CAP)
                m.then_inc(xT_ps, 1)

            def gate_or_up(r, i, E, par, t, up):
                if not up:
                    pe.wait_ge(xl_ok, E + 1)
                if not isinstance(E, int) or E > 0:
                    pe.wait_ge((gs_ok, us_ok)[up], E)
                for j in range(4):
                    m = weights_pair(r, i, t + j, lambda kk: xsp[par][:, 2 * j + kk, :], (up, up), j == 0, j == 3)
                    m.then_inc((g_f, u_f)[up] if j == 3 else pair_used, 1)

            def turn_gu(E, par):
                pe.wait_ge(gs_ok, E + 1)
                pe.wait_ge(us_ok, E + 1)
                pe.wait_ge(hf_ok, E + 1)
                for a in range(2):
                    for f in range(KF):
                        m = nc.tensor.matmul(cb[:, 1, (a * KF + f) * CAP:(a * KF + f + 1) * CAP], us[:, f, :] if a else gs[:, par, f, :],
                                             kc[:, K_SEL64:K_SEL64 + CAP], start=True, stop=True)
                m.then_inc(gt_ps, 1)

            def down(r, i, E, t, banks=(2, 3), between=None):
                pe.wait_ge(hl_ok, E + 1)
                if banks == (2, 3):
                    pe.wait_ge(yo_ok, E + 1)
                for j in range(4):
                    m = weights_pair(r, i, t + j, lambda kk: hsp[:, j, :], banks, j == 0, j == 3)
                    m.then_inc(y_f if j == 3 else pair_used, 1)
                    if j == 1 and between:
                        between()

            def moe_round(r):
                E0, n0 = r * NE, r * (NE // 2)
                pe.wait_ge(hot_ok, r + 1)
                tab = cb[0:CAP, 2, 0:NE]
                for n in range(2 * TT):
                    m = nc.tensor.matmul(tab, at_slot[:, n // TT, n % TT, :], what[:, n // TT, n % TT, :], start=n == 0, stop=n == 2 * TT - 1)
                m.then_inc(tab_ps, 1)
                turn_x(None if isinstance(r, int) else E0, 0, n0)
                gate_or_up(r, 0, E0, 0, 0, 0)
                turn_x(E0 + 1, 1, n0)
                pe.wait_ge(ww_ok, 1)
                for n in range(2 * TT):
                    m = nc.tensor.matmul(cb[0:CAP, 3, 0:NE], at_slot[:, n // TT, n % TT, :], rt[:, 1 + n // TT, (n % TT) * NE:(n % TT + 1) * NE], start=n == 0, stop=n == 2 * TT - 1)
                m.then_inc(wt_ps, 1)
                gate_or_up(r, 0, E0, 0, 4, 1)

                def expert(i, e, par, t, last):
                    E = E0 + i * 2 + e
                    turn_gu(E - 1, 1 - par)
                    gate_or_up(r, i, E, par, t, 0)
                    if not last:
                        turn_x(E + 1, 1 - par, n0 + i + (e + 1) // 2)
                    gate_or_up(r, i, E, par, t + 4, 1)
                    down(r, i, E - 1, t + 8, between=(lambda: turn_gu(E, par)) if last else None)

                with pe.Fori(0, NE // 2 - 1, 1) as i:
                    expert(i, 1, 1, 8, False)
                    expert(i, 2, 0, 20, False)
                expert(0, NE - 1, 1, 8 + E_PAIRS * (NE - 2), True)
                down(r, 0, E0 + NE - 1, R_PAIRS - 4, (0, 1))

            moe_round(0)
            pe.wait_ge(cnt_ok, 1)
            most = pe.value_load(cnt[0:1, 0:1], min_val=0, max_val=T)
            with pe.Fori(1, ROUNDS, 1) as r:
                with pe.If(most > r * CAP):
                    moe_round(r)

        @block.scalar
        def _(act):
            chain = [0]

            def own(ins):
                chain[0] += 1
                ins.then_inc(a_own, 1)
                act.wait_ge(a_own, chain[0])

            def mix_head(q):
                n = q // 2
                act.wait_ge(raw_in[n % MIX_RAW], 16 * (n // MIX_RAW + 1))
                if q >= RING:
                    wait_mix_pair(act, q - RING)
                nc.scalar.activation(wh[:, q % RING, :, :], raw_mix[n % MIX_RAW][:, 2 * (q % 2):2 * (q % 2) + 2, :], ACT.Copy).then_inc(wh_ok, 1)

            def root(n, width, c=0):
                act.wait_ge(var_ok, n + 1)
                nc.scalar.activation(stat[:, 1, c:c + width], stat[:, 0, c:c + width], ACT.Sqrt).then_inc(root_ok, 1)

            for t in range(TT):
                act.wait_ge(x_in[t], 16)
                nc.scalar.activation(rvo[:, t, :], xt[:, t, :], ACT.Square, accum_out=ssq[:, t:t + 1]).then_inc(sq_ok, 1)
            root(0, TT)
            act.wait_ge(v_own, RSTD_STEPS)
            for t in (1, 3):
                nc.scalar.activation(xs0[:, t, :], xt[:, t, :], ACT.Copy, scale=stat[:, 2, t:t + 1]).then_inc(xs_ok[1], 1)
            mix_head(0)
            mix_head(1)
            act.wait_ge(vC, 1)
            for k in range(KD):
                act.wait_ge(hT_ps, k + 1)
                nc.scalar.activation(hTh[:, k, :], (pj, cb)[k // 4][:, k % 4, :], ACT.Identity, scale=vcol[:, k:k + 1]).then_inc(hTh_ok, 1)
                if k == 4:
                    mix_head(2)
            act.wait_ge(wg_in, 48)
            act.wait_ge(zero_ok, 3)
            for a in range(2):
                nc.scalar.activation(wgh[:, :, 32 * a:32 * a + H], wgr[:, :, H * a:H * a + H], ACT.Copy).then_inc(gwh_ok, 1)

            def bank_copy(b, i, dst):
                act.wait_ge(full[i], b + 1)
                nc.scalar.activation(dst, pj[:, i, :], ACT.Copy).then_inc(free[i], 1)

            def ret_output(i):
                c, h = divmod(i, 4)
                act.wait_ge(r_o, i + 1)
                if i >= 1:
                    act.wait_ge(r_out, i)
                nc.scalar.activation(rsq[:, :], cb[:, i % 2, P:P + DV], ACT.Square, accum_out=ssq[:, i:i + 1])
                nc.scalar.activation(rvo[:, c, h * DV:(h + 1) * DV], cb[:, i % 2, P:P + DV], ACT.Copy).then_inc(r_out, 1)

            def ml_output(i):
                c, h = divmod(i, 4)
                act.wait_ge(m_rc, i + 1)
                nc.scalar.activation(mva[:, c, h, 0:DV], cb[:, i % 2, P:P + DV], ACT.Copy, scale=rden[:, i % 2:i % 2 + 1]).then_inc(m_h, 1)

            def out_head(n):
                act.wait_ge(tr_ps, n + 1)
                if n == KD:
                    wait_mix_pair(act, 4 * B_WR - 1)
                nc.scalar.activation((retTh, mixTh)[n // KD][:, n % KD, :], cb[:, n % 4, :], ACT.Identity, scale=vcol[:, 8 + n:9 + n]).then_inc(tr_h, 1)

            for b in range(BLOCKS + 1):
                p = b - 1
                for i in range(4):
                    if p == B_RQ:
                        bank_copy(p, i, rqn[:, i, :])
                    if p == B_RK:
                        bank_copy(p, i, rkn[:, i, :])
                    if p in (B_RV, B_RV + 1):
                        bank_copy(p, i, rvo[:, i, 512 * (p - B_RV):512 * (p - B_RV + 1)])
                    if p in (B_MQ, B_MK):
                        if p == B_MQ and i == 0:
                            act.wait_ge(zero_ok, 3)
                        if p == B_MK:
                            act.wait_ge(mqk_ok, i + 1)
                        bank_copy(p, i, convx[:, i, 3:3 + T])
                    if p in (B_MV, B_MV + 1):
                        h0 = 2 * (p - B_MV)
                        act.wait_ge(full[i], p + 1)
                        nc.scalar.activation(mva[:, i, h0:h0 + 2, 0:DV], pj[:, i, :].rearrange("p (h v) -> p h v", h=2), ACT.Copy).then_inc(free[i], 1)
                    if p in (B_RG, B_RG + 1):
                        n = 4 * (p - B_RG) + i
                        act.wait_ge(full[i], p + 1)
                        if n >= 4:
                            act.wait_ge(ret_ok, 2 * (n - 3))
                        nc.scalar.activation(rsg[:, n % 4, :], pj[:, i, :], ACT.Sigmoid).then_inc(rg_s, 1)
                    if p in (B_GR, B_GR + 1, B_GM, B_GM + 1):
                        dst, ct = (mrg, 4 * (p - B_GR) + i) if p < B_GM else (sgm, 4 * (p - B_GM) + i)
                        act.wait_ge(full[i], p + 1)
                        if p == B_GR and i == 0:
                            act.wait_ge(ret_ok, 16)
                        nc.scalar.activation(dst[:, ct, :], pj[:, i, :], ACT.Sigmoid).then_inc(free[i], 1)
                    if p in (B_MO, B_MO + 1):
                        n = 4 * (p - B_MO) + i
                        act.wait_ge(full[i], p + 1)
                        if n == 0:
                            act.wait_ge(tr_ps, KD)
                        if n >= 2:
                            act.wait_ge(mo_v, n - 1)
                        nc.scalar.activation(msg[:, n % 2, :], pj[:, i, :], ACT.Sigmoid).then_inc(free[i], 1)
                    if p in (B_WM, B_WM + 1):
                        ct = 4 * (p - B_WM) + i
                        act.wait_ge(mg_ok, ct + 1)
                        if ct == 0:
                            wait_mix_pair(act, 4 * B_WM - 1)
                        nc.scalar.activation(mrgTh[:, ct, :], mrg[:, ct, :], ACT.Copy).then_inc(mgh_ok, 1)
                if b == BLOCKS:
                    break
                if b == B_RV:
                    act.wait_ge(g_ps, 1)
                    nc.scalar.activation(grow[:, 0, :], cb[0:H, 3, :], ACT.Identity, bias=bif[:, 0:1]).then_inc(grow_a, 1)
                    nc.scalar.activation(grow[:, 1, :], cb[32:32 + H, 3, :], ACT.Copy).then_inc(grow_a, 1)
                    act.wait_ge(f_abs, 1)
                    own(nc.scalar.activation(grow[:, 2, :], grow[:, 2, :], ACT.Exp, scale=-1.0))
                    nc.scalar.activation(grow[:, 2, :], grow[:, 2, :], ACT.Ln, bias=1.0).then_inc(f_log, 1)
                if b == B_MQ:
                    act.wait_ge(gex_in, 1)
                    nc.scalar.activation(gex[:, :, :], gex[:, :, :], ACT.Exp).then_inc(gex_ok, 1)
                if b == B_RG:
                    ret_output(15)
                    root(1, 16)
                for j in range(4):
                    q = 4 * b + j
                    i = 4 * (b - B_MQ) + j
                    if 0 < i < 16:
                        ret_output(i - 1)
                    i = 4 * (b - B_RG) + j
                    if 0 < i < 17:
                        ml_output(i - 1)
                    if q + LEAD < MIX_PAIRS:
                        mix_head(q + LEAD)
                    if b == B_RV + 1:
                        act.wait_ge(rkT_ps, j + 1)
                        nc.scalar.activation(rkT[:, :, j * P:(j + 1) * P], cb[:, j, :].rearrange("p (h l) -> p h l", h=H), ACT.Copy).then_inc(rkT_ok, 1)
                        for h in ((), (0,), (1,), (2, 3))[j]:
                            act.wait_ge(gb_ps, h + 1)
                            nc.scalar.activation(gbc[:, h, :], cb[:, h, :], ACT.Copy).then_inc(gb_ok, 1)
                    if b == B_MQ:
                        act.wait_ge(dt_in, j + 1)
                        nc.scalar.activation(dT[:, j, :], dT[:, j, :], ACT.Exp, scale=-1.0).then_inc(dt_ok, 1)
                        for c in range(TT):
                            m = nc.scalar.activation(gbc[:, j, c * P:(c + 1) * P], gbc[:, j, c * P:(c + 1) * P], ACT.Exp, scale=-1.0,
                                                     bias=gcol[:, 3, 4 * j + c:4 * j + c + 1])
                        m.then_inc(wint_ok, 1)
                    if b in (B_MQ + 1, B_MK + 1):
                        n = 4 * (b - B_MQ - 1) + j
                        dst = (mqT, mkT)[n // 4]
                        act.wait_ge(free[j], b)
                        nc.scalar.activation(dst[:, j, :], convx[:, j, 3:3 + T], ACT.Identity, scale=vcol[:, 56 + n:57 + n], bias=vcol[:, 24 + n:25 + n]).then_inc(conv_a, 1)
                        act.wait_ge(conv_v, n + 1)
                        if n >= 1:
                            act.wait_ge(mqk_ok, n)
                        nc.scalar.activation(csg[:, :], dst[:, j, :], ACT.Sigmoid).then_inc(conv_s, 1)
                    if B_RG <= b < B_GM:
                        i = 4 * (b - B_RG) + j
                        act.wait_ge(m_s, i + 1)
                        if i >= 2:
                            act.wait_ge(m_o, i - 1)
                        nc.scalar.activation(wk[:, i % 2, :], cb[:, 2 + i % 2, 0:P], ACT.Copy, scale=gex[:, 1, i:i + 1]).then_inc(m_wk, 1)
                    if b in (B_MO + 1, B_MO + 2) and j < 2:
                        h = 2 * (b - B_MO - 1)
                        for t in (2 * j, 2 * j + 1):
                            n = 4 * (b - B_MO - 1) + t
                            act.wait_ge(mo_v, n + 1)
                            for a in range(2):
                                m = nc.scalar.activation(rsq[:, :], mva[:, t, h + a, 0:DV], ACT.Square, accum_out=ssq[:, 4 * (h + a) + t:4 * (h + a) + t + 1])
                                if a == 0:
                                    own(m)
                            m.then_inc(sq_ok, 1)
                            act.wait_ge(sq_ok, TT + n + 1)
                    if b in (B_GM, B_GM + 1):
                        out_head(4 * (b - B_GM) + j)
                    if b in (B_WR, B_WR + 1):
                        out_head(8 + 4 * (b - B_WR) + j)
                    if b in (B_MO + 1, B_MO + 2) and j == 2:
                        root(2 + b - B_MO - 1, 8)

            def square(t):
                act.wait_ge(free[t], BLOCKS)
                nc.scalar.activation(h2[:, t, :], x2[:, t, :], ACT.Square, accum_out=ssq[:, t:t + 1]).then_inc(sq_ok, 1)

            def stream_copy(t):
                act.wait_ge(h2T_ps, 2 * t + 2)
                bank = cb[:, 2 * t + 1, :] if t < 2 else pj[:, 2 * t + 1 - TT, :]
                nc.scalar.activation(h2T[:, 4:8, t * P:(t + 1) * P], bank.rearrange("p (k n) -> p k n", k=4), ACT.Copy).then_inc(h2T_a, 1)

            square(0)
            square(1)
            stream_copy(0)
            square(2)
            stream_copy(1)
            square(3)
            root(4, TT)
            stream_copy(2)
            stream_copy(3)
            for t in range(TT):
                act.wait_ge(h2_ok, t + 1)
                act.dma_start(h_dram[t * P:(t + 1) * P, :], h2[:, t, :]).then_inc(h2_out, 16)
            act.wait_ge(e1_in, 1)
            nc.scalar.activation(rt[:, 5, 0:TT * NG], rt[:, 5, 0:TT * NG], ACT.Exp).then_inc(e1_ok, 1)
            act.wait_ge(e2_in, 1)
            nc.scalar.activation(rt[:, 6, 0:TT], rt[:, 6, 0:TT], ACT.Exp).then_inc(e2_ok, 1)
            act.wait_ge(e2_ok, 1)
            nc.scalar.activation(stat[:, 1, 0:TT], rt[:, 6, 0:TT], ACT.Sigmoid)

            def head(r, i, t):
                src, s, loads = moe_raw(t)
                act.wait_ge(moe_in[s], r * (16 * LOADS) + i * 16 + 16 * loads)
                wait_pair_used(act, r, i, t)
                nc.scalar.activation(moe_split(wh, wh_more, t), src, ACT.Copy).then_inc(wh_ok, 1)

            def x_head(E, par):
                act.wait_ge(xT_ps, E + 1)
                nc.scalar.activation(xsp[par][:, :, 0:CAP], cb[:, 0, :].rearrange("p (k n) -> p k n", k=KD), ACT.Copy).then_inc(xh_ok, 1)

            def gate_copy(E, par):
                act.wait_ge(g_f, E + 1)
                nc.scalar.activation(gs[:, par, :, :], pj[:, 0, :].rearrange("p (m f) -> p f m", f=KF), ACT.Copy).then_inc(gs_ok, 1)

            def gate_sigmoid(E):
                act.wait_ge(gt_ps, E + 1)
                nc.scalar.activation(sg[:, :], cb[:, 1, 0:KF * CAP], ACT.Sigmoid).then_inc(sg_ok, 1)

            def hidden_head(E):
                act.wait_ge(hf_ok, E + 2)
                if not isinstance(E, int) or E > 0:
                    act.wait_ge(y_f, E)
                nc.scalar.activation(hsp[:, :, 0:CAP], hf[:, :].rearrange("p (f n) -> p f n", f=KF), ACT.Copy).then_inc(hh_ok, 1)

            def y_tails(E, bank=2):
                act.wait_ge(y_f, E + 1)
                act.wait_ge(yo_ok, E + 1)
                nc.scalar.activation(yb[:, :].rearrange("p (a n) -> p a n", a=2), pj[CAP:P, bank:bank + 2, :], ACT.Copy).then_inc(yb_ok, 1)

            def y_weight(E, par):
                act.wait_ge(w_c, E + 1)
                act.wait_ge(yo_ok, E + 2)
                nc.scalar.activation(yo[:, par, :], yo[:, par, :], ACT.Copy, scale=w_now[:, par:par + 1]).then_inc(yw_ok, 1)

            def up_copy(E):
                act.wait_ge(u_f, E + 1)
                nc.scalar.activation(us[:, :, :], pj[:, 1, :].rearrange("p (m f) -> p f m", f=KF), ACT.Copy).then_inc(us_ok, 1)

            def moe_round(r):
                E0 = r * NE
                for t in range(MOE_LEAD):
                    head(r, 0, t)
                x_head(E0, 0)
                for t in range(8):
                    head(r, 0, t + MOE_LEAD)
                    if t == 4:
                        gate_copy(E0, 0)
                        x_head(E0 + 1, 1)
                up_copy(E0)

                def expert(i, e, par, t, first=False, last=False):
                    E = E0 + i * 2 + e
                    for s in range(E_PAIRS):
                        if t + s + MOE_LEAD < R_PAIRS:
                            head(r, i, t + s + MOE_LEAD)
                        if s == 0 and not first:
                            y_tails(E - 2)
                        if s == 1:
                            gate_sigmoid(E - 1)
                        if s == 3:
                            hidden_head(E - 1)
                        if s == 4:
                            gate_copy(E, par)
                        if s == 5 and not first:
                            y_weight(E - 2, par)
                        if s == 7 and not last:
                            x_head(E + 1, 1 - par)
                        if s == (6 if last else 9):
                            up_copy(E)

                expert(0, 1, 1, 8, first=True)
                with act.Fori(0, NE // 2 - 2, 1) as i:
                    expert(i, 2, 0, 8 + E_PAIRS)
                    expert(i, 3, 1, 8 + 2 * E_PAIRS)
                expert(0, NE - 2, 0, 8 + E_PAIRS * (NE - 3))
                expert(0, NE - 1, 1, 8 + E_PAIRS * (NE - 2), last=True)
                gate_sigmoid(E0 + NE - 1)
                hidden_head(E0 + NE - 1)
                y_tails(E0 + NE - 2)
                y_weight(E0 + NE - 2, 0)
                y_tails(E0 + NE - 1, 0)
                y_weight(E0 + NE - 1, 1)

            moe_round(0)
            act.wait_ge(cnt_ok, 1)
            most = act.value_load(cnt[0:1, 0:1], min_val=0, max_val=T)
            with act.Fori(1, ROUNDS, 1) as r:
                with act.If(most > r * CAP):
                    moe_round(r)

            nc.scalar.activation(stat[:, 1, 0:TT], stat[:, 0, 0:TT], ACT.Sqrt)
            for t in range(TT):
                act.wait_ge(x3_in[t], 16)
                nc.scalar.activation(h2[:, t, :], x2[:, t, :], ACT.Square, accum_out=ssq[:, t:t + 1]).then_inc(sq_ok, 1)
                root(5 + t, 1, t)

        @block.vector
        def _(dve):
            chain = [0]

            def own(ins):
                chain[0] += 1
                ins.then_inc(v_own, 1)
                dve.wait_ge(v_own, chain[0])

            V = nc.vector

            def mix_tail(q):
                dve.wait_ge(wh_ok, q + 1)
                n = q // 2
                V.tensor_tensor(wl[:, q % RING, :, :], raw_mix[n % MIX_RAW][:, 2 * (q % 2):2 * (q % 2) + 2, :],
                                wh[:, q % RING, :, :].bitcast(F32), ALU.subtract).then_inc(wl_ok, 1)

            def rstd(n, squares, width, dim, c=0):
                v, s, y, z = (stat[:, a, c:c + width] for a in range(4))
                V.tensor_scalar(v, squares, 1.0 / dim, EPS, ALU.mult, ALU.add).then_inc(var_ok, 1)
                dve.wait_ge(root_ok, n + 1)
                own(V.reciprocal(y, s))
                own(V.tensor_tensor(z, y, y, ALU.mult))
                dve.wait_ge(var_ok, n + 1)
                own(V.tensor_tensor(z, z, v, ALU.mult))
                own(V.tensor_scalar(z, z, -0.5, 1.5, ALU.mult, ALU.add))
                own(V.tensor_tensor(y, y, z, ALU.mult))

            dve.wait_ge(sq_ok, TT)
            rstd(0, ssq[:, 0:TT], TT, D)
            for t in (0, 2):
                V.tensor_scalar(xs0[:, t, :], xt[:, t, :], stat[:, 2, t:t + 1], None, ALU.mult).then_inc(xs_ok[0], 1)
                if t == 0:
                    dve.wait_ge(vT, 1)
                    V.tensor_copy(vcol[:, :], cb[:, 3, 0:64]).then_inc(vC, 1)
            dve.wait_ge(vC, 1)
            mix_tail(0)
            mix_tail(1)
            for k in range(KD):
                dve.wait_ge(hTh_ok, k + 1)
                V.scalar_tensor_tensor(hTl[:, k, :], (pj, cb)[k // 4][:, k % 4, :], vcol[:, k:k + 1], hTh[:, k, :].bitcast(F32), ALU.mult, ALU.subtract).then_inc(hTl_ok, 1)
                if k == 5:
                    mix_tail(2)
            for a in range(2):
                dve.wait_ge(gwh_ok, a + 1)
                V.tensor_tensor(wgl[:, :, 32 * a:32 * a + H], wgr[:, :, H * a:H * a + H], wgh[:, :, 32 * a:32 * a + H].bitcast(F32), ALU.subtract).then_inc(gwl_ok, 1)

            def rq_turned(t):
                dve.wait_ge(rqT_ps, t + 1)
                V.tensor_tensor(rqT[:, :, t * P:(t + 1) * P], cb[:, t, :].rearrange("p (h l) -> p h l", h=H),
                                kc[:, K_QDEC:K_QDEC + H * P].rearrange("p (h l) -> p h l", h=H), ALU.mult).then_inc(rqT_ok, 1)

            def ret_masked(i):
                dve.wait_ge(r_s, i + 1)
                V.tensor_tensor(st[:, i % 2, :], cb[:, i % 2, 0:P], kc[:, K_RMASK + (i % 4) * P:K_RMASK + (i % 4 + 1) * P], ALU.mult).then_inc(r_st, 1)

            def ret_state(i):
                c, h = divmod(i, 4)
                if c == TT - 1:
                    return
                dve.wait_ge(r_o, i + 1)
                if c == 0:
                    V.tensor_copy(Rst[:, h, :], cb[:, 2 + i % 2, 0:DV]).then_inc(r_R, 1)
                else:
                    V.scalar_tensor_tensor(Rst[:, h, :], Rst[:, h, :], GAMMA[h] ** P, cb[:, 2 + i % 2, 0:DV], ALU.mult, ALU.add).then_inc(r_R, 1)

            def ml_weighted(i):
                c, h = divmod(i, 4)
                dve.wait_ge(m_s, i + 1)
                V.tensor_tensor(st[:, i % 2, :], cb[:, i % 2, 0:P], dT[:, h, c * P:(c + 1) * P], ALU.mult).then_inc(m_st, 1)

            def ml_state(i):
                c, h = divmod(i, 4)
                dve.wait_ge(m_o, i + 1)
                if i >= 2:
                    dve.wait_ge(m_h, i - 1)
                den, tmp = cb[:, i % 2, P + DV:P + DA], rden[:, i % 2:i % 2 + 1]
                own(V.tensor_scalar(tmp, den, -1.0, gex[:, 0, i:i + 1], ALU.mult, ALU.max))
                own(V.tensor_tensor(tmp, den, tmp, ALU.max))
                V.reciprocal(tmp, tmp).then_inc(m_rc, 1)
                if c == 0:
                    V.tensor_copy(Cst[:, h, :], cb[:, 2 + i % 2, P:P + DA]).then_inc(m_C, 1)
                elif c < TT - 1:
                    V.scalar_tensor_tensor(Cst[:, h, :], Cst[:, h, :], gex[:, 2, i:i + 1], cb[:, 2 + i % 2, P:P + DA], ALU.mult, ALU.add).then_inc(m_C, 1)

            def merged_tail(ct):
                dve.wait_ge(mgh_ok, ct + 1)
                V.tensor_tensor(mrgTl[:, ct, :], mrg[:, ct, :], mrgTh[:, ct, :].bitcast(F32), ALU.subtract).then_inc(mgl_ok, 1)

            def out_tail(n):
                dve.wait_ge(tr_h, n + 1)
                V.scalar_tensor_tensor((retTl, mixTl)[n // KD][:, n % KD, :], cb[:, n % 4, :], vcol[:, 8 + n:9 + n],
                                       (retTh, mixTh)[n // KD][:, n % KD, :].bitcast(F32), ALU.mult, ALU.subtract).then_inc(tr_l, 1)

            for b in range(BLOCKS + 1):
                p = b - 1
                for i in range(4):
                    if p in (B_RG, B_RG + 1):
                        n = 4 * (p - B_RG) + i
                        dve.wait_ge(rg_s, n + 1)
                        V.tensor_tensor(rsg[:, i, :], pj[:, i, :], rsg[:, i, :], ALU.mult).then_inc(free[i], 1)
                    if p in (B_MO, B_MO + 1):
                        n, h0 = 4 * (p - B_MO) + i, 2 * (p - B_MO)
                        dve.wait_ge(free[i], p + 1)
                        V.tensor_tensor(mva[:, i, h0:h0 + 2, 0:DV], mva[:, i, h0:h0 + 2, 0:DV],
                                        msg[:, n % 2, :].rearrange("p (h v) -> p h v", h=2), ALU.mult).then_inc(mo_v, 1)
                    if p in (B_WR, B_WR + 1):
                        ct = 4 * (p - B_WR) + i
                        dve.wait_ge(full[i], p + 1)
                        V.tensor_tensor(mrg[:, ct, :], pj[:, i, :], mrg[:, ct, :], ALU.mult).then_inc(free[i], 1)
                    if p in (B_WM, B_WM + 1):
                        ct = 4 * (p - B_WM) + i
                        dve.wait_ge(full[i], p + 1)
                        V.tensor_tensor(sgm[:, ct, :], pj[:, i, :], sgm[:, ct, :], ALU.mult).then_inc(free[i], 1)
                    if p in (B_WO, B_WO + 1):
                        half = slice(512 * (p - B_WO), 512 * (p - B_WO + 1))
                        if p == B_WO and i == 0:
                            dve.wait_ge(xr_in, 16)
                        dve.wait_ge(full[i], p + 1)
                        V.tensor_tensor(x2[:, i, half], pj[:, i, :], x2[:, i, half], ALU.add).then_inc(free[i], 1)
                if p in (B_WM, B_WM + 1):
                    for i in range(4):
                        ct = 4 * (p - B_WM) + i
                        dve.wait_ge(free[i], p + 1)
                        V.tensor_tensor(mrg[:, ct, :], mrg[:, ct, :], sgm[:, ct, :], ALU.add).then_inc(mg_ok, 1)
                        if i >= 1:
                            merged_tail(ct - 1)
                    merged_tail(ct)
                if b == BLOCKS:
                    break
                if b == B_WO + 1:
                    dve.wait_ge(br_in, 80)
                    V.tensor_tensor(wrt[:, :, :], wrt[:, :, :], nwc[:, :].unsqueeze(2).to_broadcast([P, KD, 36]), ALU.mult).then_inc(wrt_ok, 1)
                if b == B_RV:
                    dve.wait_ge(grow_a, 2)
                    own(V.tensor_scalar(grow[:, 1, :], grow[:, 1, :], bif[:, 1:2], None, ALU.add))
                    V.scalar_tensor_tensor(grow[:, 2, :], grow[:, 1, :], -1.0, grow[:, 1, :], ALU.mult, ALU.max).then_inc(f_abs, 1)
                    dve.wait_ge(f_log, 1)
                    own(V.scalar_tensor_tensor(grow[:, 1, :], grow[:, 1, :], 0.0, grow[:, 2, :], ALU.min, ALU.subtract))
                    for c in range(TT):
                        cs = slice(c * P, (c + 1) * P)
                        m = V.tensor_tensor_scan(grow[:, 2, cs], onesq[0:H, :], grow[:, 1, cs], 0.0, ALU.mult, ALU.add)
                    own(m)
                    own(V.tensor_tensor(grow[:, 3, :], grow[:, 0, :], grow[:, 2, :], ALU.subtract))
                    own(V.memset(mprev[:, 0:1], 0.0))
                    for c in range(TT):
                        cs, end = slice(c * P, (c + 1) * P), (c + 1) * P - 1
                        own(V.tensor_tensor_scan(grow[:, 4, cs], grow[:, 3, cs], grow[:, 3, cs], mprev[:, c:c + 1], ALU.max, ALU.max))
                        m = V.tensor_tensor(mprev[:, c + 1:c + 2], grow[:, 2, end:end + 1], grow[:, 4, end:end + 1], ALU.add)
                        if c < TT - 1:
                            own(m)
                    m.then_inc(grow_ok, 1)
                if b == B_RV + 1:
                    dve.wait_ge(gtiny, 1)
                    V.tensor_copy(gcol[:, :, :], cb[:, 3, 0:80].rearrange("p (a n) -> p a n", a=5)).then_inc(gcol_ok, 1)
                    dve.wait_ge(gcol_ok, 1)
                    last = gcol[:, 4, :].rearrange("p (h c) -> p c h", h=H)
                    V.scalar_tensor_tensor(gex[:, 0, :], gcol[:, 1, :], -1.0, gcol[:, 2, :], ALU.mult, ALU.subtract)
                    V.tensor_tensor(gex[:, 1, :].rearrange("p (c h) -> p c h", h=H), gcol[:, 0, :].rearrange("p (c h) -> p c h", h=H), last, ALU.subtract)
                    V.tensor_tensor(gex[:, 2, :].rearrange("p (c h) -> p c h", h=H), gcol[:, 3, :].rearrange("p (h c) -> p c h", h=H), last, ALU.subtract).then_inc(gex_in, 1)
                if b == B_RG:
                    dve.wait_ge(r_out, 16)
                    rstd(1, ssq[:, :], 16, DV)
                    own(V.tensor_copy(rret[:, :], stat[:, 2, :]))
                    dve.wait_ge(gex_ok, 1)
                for j in range(4):
                    q = 4 * b + j
                    i = 4 * (b - B_MQ) + j
                    if 0 < i < 16:
                        ret_state(i - 1)
                    i = 4 * (b - B_RG) + j
                    if 0 < i < 17:
                        ml_state(i - 1)
                    if q + LEAD < MIX_PAIRS:
                        mix_tail(q + LEAD)
                    if b == B_RV:
                        if j >= 1:
                            rq_turned(j - 1)
                    if b == B_MQ:
                        dve.wait_ge(gb_ok, j + 1)
                        for c in range(TT):
                            m = V.scalar_tensor_tensor(dT[:, j, c * P:(c + 1) * P], gbc[:, j, c * P:(c + 1) * P], gcol[:, 0, 4 * c + j:4 * c + j + 1],
                                                       kc[:, K_NOTYET:K_NOTYET + P], ALU.subtract, ALU.add)
                        m.then_inc(dt_in, 1)
                    if B_MQ <= b < B_RG:
                        ret_masked(4 * (b - B_MQ) + j)
                    if b in (B_MQ + 1, B_MK + 1):
                        n = 4 * (b - B_MQ - 1) + j
                        dst = (mqT, mkT)[n // 4][:, j, :]
                        dve.wait_ge(conv_a, n + 1)
                        for tap in range(3):
                            m = V.scalar_tensor_tensor(dst, convx[:, j, tap:tap + T], vcol[:, 32 + 8 * tap + n:33 + 8 * tap + n], dst, ALU.mult, ALU.add)
                            if tap < 2:
                                own(m)
                        m.then_inc(conv_v, 1)
                        dve.wait_ge(conv_s, n + 1)
                        V.scalar_tensor_tensor(dst, dst, (1.0, DK ** -0.5)[n // 4], csg[:, :], ALU.mult, ALU.mult).then_inc(mqk_ok, 1)
                    if b == B_MV + 1:
                        if j == 0:
                            dve.wait_ge(mqk_ok, 8)
                        dve.wait_ge(wint_ok, j + 1)
                        V.tensor_tensor(gbc[:, j, :], gbc[:, j, :], mqT[:, j, :], ALU.mult).then_inc(wq_ok, 1)
                    if B_RG <= b < B_GM:
                        if b == B_RG and j == 0:
                            dve.wait_ge(dt_ok, H)
                        ml_weighted(4 * (b - B_RG) + j)
                    if b in (B_GM, B_GM + 1):
                        out_tail(4 * (b - B_GM) + j)
                    if b in (B_WR, B_WR + 1):
                        out_tail(8 + 4 * (b - B_WR) + j)
                    if p in (B_RG, B_RG + 1):
                        dve.wait_ge(free[j], p + 1)
                        for a in range(2):
                            h = 2 * (p - B_RG) + a
                            V.scalar_tensor_tensor(rvo[:, j, h * DV:(h + 1) * DV], rvo[:, j, h * DV:(h + 1) * DV], rret[:, 4 * j + h:4 * j + h + 1],
                                                   rsg[:, j, a * DV:(a + 1) * DV], ALU.mult, ALU.mult).then_inc(ret_ok, 1)
                    if b in (B_MO + 1, B_MO + 2) and j == 2:
                        half = b - B_MO - 1
                        dve.wait_ge(sq_ok, TT * (2 + half))
                        rstd(2 + half, ssq[:, 8 * half:8 * half + 8], 8, DV)
                        for t in range(TT):
                            for a in range(2):
                                hv = mva[:, t, 2 * half + a, 0:DV]
                                m = V.tensor_scalar(hv, hv, stat[:, 2, 4 * a + t:4 * a + t + 1], None, ALU.mult)
                        m.then_inc(hm_ok, 1)
                if b == B_RV:
                    rq_turned(3)

            for t in range(TT):
                dve.wait_ge(h2T_ps, 2 * t + 1)
                bank = cb[:, 2 * t, :] if t < 2 else pj[:, 2 * t - TT, :]
                V.tensor_copy(h2T[:, 0:4, t * P:(t + 1) * P], bank.rearrange("p (k n) -> p k n", k=4)).then_inc(h2T_v, 1)
            dve.wait_ge(sq_ok, 4 * TT)
            rstd(4, ssq[:, 0:TT], TT, D)
            dve.wait_ge(wr_in, 16)
            for t in range(TT):
                V.scalar_tensor_tensor(h2[:, t, :].rearrange("q (k p) -> q k p", k=KD), x2[:, t, :].rearrange("q (p k) -> q k p", k=KD), stat[:, 2, t:t + 1],
                                       wrow[:, :].rearrange("q (p k) -> q k p", k=KD), ALU.mult, ALU.mult).then_inc(h2_ok, 1)
            V.memset(ones16[:, :], 1.0)
            V.tensor_copy(before16[:, :], kc[:, K_BEFORE:K_BEFORE + P])

            def tiles(a, n):
                return rt[:, a, 0:TT * n].rearrange("p (t n) -> p t n", n=n)

            def first_best(score, best, n, a_, b_):
                x_, y_ = tiles(a_, n), rt[:, b_, 0:TT]
                own(V.tensor_tensor(x_, score, best.unsqueeze(2).to_broadcast([P, TT, n]), ALU.is_equal))
                own(V.tensor_tensor(x_, x_, kc[:, K_PRIO + NE - n:K_PRIO + NE].unsqueeze(1).to_broadcast([P, TT, n]), ALU.mult))
                own(V.reduce_max(y_, x_, AX.X))
                own(V.tensor_tensor(x_, x_, y_.unsqueeze(2).to_broadcast([P, TT, n]), ALU.is_equal))

            dve.wait_ge(lg_ps, 1)
            for t in range(TT):
                m = V.scalar_tensor_tensor(lg[:, t, :], cb[:, 0, t * 36:(t + 1) * 36], stat[:, 2, t:t + 1], brt[:, :], ALU.mult, ALU.add)
            own(m)
            gl, el = lg[:, :, 0:NG], lg[:, :, NG:36]
            gmax = rt[:, 7, 0:TT]
            own(V.reduce_max(gmax, gl, AX.X))
            V.tensor_tensor(tiles(5, NG), gl, gmax.unsqueeze(2).to_broadcast([P, TT, NG]), ALU.subtract).then_inc(e1_in, 1)
            first_best(gl, gmax, NG, 3, 4)
            own(V.tensor_scalar(tiles(3, NG), tiles(3, NG), -1.0, BIG, ALU.add, ALU.mult))
            own(V.tensor_tensor(el.rearrange("p t (g e) -> p t g e", g=NG), el.rearrange("p t (g e) -> p t g e", g=NG),
                                tiles(3, NG).unsqueeze(3).to_broadcast([P, TT, NG, EG]), ALU.add))
            m1, m2 = rt[:, 7, 8:8 + TT], rt[:, 7, 16:16 + TT]
            own(V.reduce_max(m1, el, AX.X))
            first_best(el, m1, NE, 1, 4)
            own(V.scalar_tensor_tensor(el, tiles(1, NE), -2 * BIG, el, ALU.mult, ALU.add))
            own(V.reduce_max(m2, el, AX.X))
            V.tensor_tensor(rt[:, 6, 0:TT], m2, m1, ALU.subtract).then_inc(e2_in, 1)
            first_best(el, m2, NE, 2, 4)
            V.tensor_tensor(hot16[:, :], rt[:, 1, :], rt[:, 2, :], ALU.add).then_inc(hot_in, 1)
            for k in range(2):
                V.tensor_tensor(what[:, k, :, :], tiles(1 + k, NE), kc[:, K_TOK:K_TOK + TT].unsqueeze(2).to_broadcast([P, TT, NE]), ALU.mult)
            dve.wait_ge(pos_ps, 1)
            ppos = cb[:, 1, 0:TT * NE].rearrange("p (t e) -> p t e", e=NE)
            for k in range(2):
                m = V.tensor_tensor(tiles(3 + k, NE), ppos, tiles(1 + k, NE), ALU.mult)
            own(m)
            for k in range(2):
                m = V.reduce_sum(pos[:, k, :], tiles(3 + k, NE), AX.X)
            own(m)

            def weights():
                own(V.reduce_max(rt[:, 7, 40:41], cb[:, 1, TT * NE:(TT + 1) * NE], AX.X))
                V.tensor_copy(cnt[:, :], rt[0:1, 7, 40:41]).then_inc(cnt_ok, 1)
                dve.wait_ge(e1_ok, 1)
                gw, ee, dd = rt[:, 7, 24:24 + TT], rt[:, 6, 0:TT], rt[:, 7, 32:32 + TT]
                own(V.reduce_sum(gw, tiles(5, NG), AX.X))
                dve.wait_ge(e2_ok, 1)
                own(V.tensor_scalar(dd, ee, 1.0, None, ALU.add))
                own(V.tensor_tensor(dd, dd, gw, ALU.mult))
                own(V.reciprocal(slotw[:, 0, :], dd))
                own(V.tensor_tensor(slotw[:, 1, :], slotw[:, 0, :], ee, ALU.mult))
                for k in range(2):
                    m = V.tensor_tensor(tiles(1 + k, NE), tiles(1 + k, NE), slotw[:, k, :].unsqueeze(2).to_broadcast([P, TT, NE]), ALU.mult)
                m.then_inc(ww_ok, 1)

            dve.sem_inc(hf_ok, 1)
            dve.sem_inc(yo_ok, 1)

            def tail(r, i, t):
                if t % E_PAIRS == POOL_PAIR or t >= R_PAIRS:
                    return
                src, s, loads = moe_raw(t)
                dve.wait_ge(wh_ok, r * R_PAIRS + i * 24 + (MIX_PAIRS + t + 1))
                V.tensor_tensor(moe_split(wl, wl_more, t), src, moe_split(wh, wh_more, t).bitcast(F32), ALU.subtract).then_inc(wl_ok, 1)

            def x_tail(E, par):
                dve.wait_ge(xh_ok, E + 1)
                V.tensor_tensor(xsp[par][:, :, CAP:P], cb[:, 0, :].rearrange("p (k n) -> p k n", k=KD), xsp[par][:, :, 0:CAP].bitcast(F32), ALU.subtract).then_inc(xl_ok, 1)

            def hidden(E):
                dve.wait_ge(sg_ok, E + 1)
                V.tensor_tensor(sg[:, :], cb[:, 1, 0:KF * CAP], sg[:, :], ALU.mult).then_inc(hq_ok, 1)
                dve.wait_ge(hq_ok, E + 1)
                V.tensor_tensor(hf[:, :], cb[:, 1, KF * CAP:2 * KF * CAP], sg[:, :], ALU.mult).then_inc(hf_ok, 1)

            def hidden_tail(E):
                dve.wait_ge(hh_ok, E + 1)
                V.tensor_tensor(hsp[:, :, CAP:P], hf[:, :].rearrange("p (f n) -> p f n", f=KF), hsp[:, :, 0:CAP].bitcast(F32), ALU.subtract).then_inc(hl_ok, 1)

            def y_sum(E, par, bank=2):
                dve.wait_ge(yb_ok, E + 1)
                dve.wait_ge(out_ok, E + 1)
                V.tensor_tensor(yo[:, par, :].rearrange("p (a n) -> p a n", a=2), pj[0:CAP, bank:bank + 2, :], yb[:, :].rearrange("p (a n) -> p a n", a=2), ALU.add).then_inc(yo_ok, 1)

            def moe_round(r):
                E0, n0 = r * NE, r * (NE // 2)
                if not isinstance(r, int):
                    dve.wait_ge(r_done, r)
                    dve.wait_ge(it_ok, r)
                    V.tensor_scalar(iot[:, :], iot[:, :], float(CAP), None, ALU.add).then_inc(it_ok, 1)
                    dve.wait_ge(it_ok, r + 1)
                else:
                    V.tensor_copy(iot[:, :], kc[:, K_SLOT:K_SLOT + CAP]).then_inc(it_ok, 1)
                    dve.wait_ge(it_ok, 1)
                V.tensor_tensor(at_slot[:, :, :, :].rearrange("p k t s -> p (k t) s"), pos[:, :, :].rearrange("p k t -> p (k t)").unsqueeze(2).to_broadcast([P, 2 * TT, CAP]),
                                iot[:, :].unsqueeze(1).to_broadcast([P, 2 * TT, CAP]), ALU.is_equal).then_inc(hot_ok, 1)
                tail(r, 0, 0)
                dve.wait_ge(tab_ps, r + 1)
                V.tensor_scalar(tok_tab[:, :], cb[0:CAP, 2, 0:NE], float(NO_TOKEN), None, ALU.add).then_inc(tab_ok, 1)
                if isinstance(r, int):
                    weights()
                for t in range(1, MOE_LEAD - 1):
                    tail(r, 0, t)
                x_tail(E0, 0)
                tail(r, 0, MOE_LEAD - 1)
                for t in range(8):
                    tail(r, 0, t + MOE_LEAD)
                    if t == 4:
                        x_tail(E0 + 1, 1)
                dve.wait_ge(wt_ps, r + 1)
                V.tensor_copy(w_tab[:, :], cb[0:CAP, 3, 0:NE]).then_inc(wt_ok, 1)

                def expert(i, e, par, t, first=False, last=False):
                    E = E0 + i * 2 + e
                    for s in range(E_PAIRS):
                        tail(r, i, t + s + MOE_LEAD)
                        if s == 0 and not first:
                            y_sum(E - 2, par)
                        if s == 1:
                            hidden(E - 1)
                        if s == 4:
                            hidden_tail(E - 1)
                        if s == 8 and not last:
                            x_tail(E + 1, 1 - par)

                expert(0, 1, 1, 8, first=True)
                with dve.Fori(0, NE // 2 - 2, 1) as i:
                    expert(i, 2, 0, 8 + E_PAIRS)
                    expert(i, 3, 1, 8 + 2 * E_PAIRS)
                expert(0, NE - 2, 0, 8 + E_PAIRS * (NE - 3))
                expert(0, NE - 1, 1, 8 + E_PAIRS * (NE - 2), last=True)
                hidden(E0 + NE - 1)
                hidden_tail(E0 + NE - 1)
                y_sum(E0 + NE - 2, 0)
                y_sum(E0 + NE - 1, 1, 0)

            moe_round(0)
            dve.wait_ge(cnt_ok, 1)
            most = dve.value_load(cnt[0:1, 0:1], min_val=0, max_val=T)
            with dve.Fori(1, ROUNDS, 1) as r:
                with dve.If(most > r * CAP):
                    moe_round(r)

            dve.wait_ge(wr_in, 32)
            for t in range(TT):
                dve.wait_ge(sq_ok, 4 * TT + t + 1)
                rstd(5 + t, ssq[:, t:t + 1], 1, D, t)
                V.scalar_tensor_tensor(x2[:, t, :], x2[:, t, :], stat[:, 2, t:t + 1], wrow[:, :], ALU.mult, ALU.mult).then_inc(fin_ok, 1)

        @block.gpsimd
        def _(pool):
            pool.memset(onesq[:, :], 1.0).then_inc(zero_ok, 1)
            pool.sem_inc(out_ok, 2)
            pool.wait_ge(hTl_ok, KD)
            pool.memset(wgh[:, :, :].bitcast(F32), 0.0).then_inc(zero_ok, 1)
            pool.memset(convx[:, :, 0:3], 0.0)
            pool.memset(mva[:, :, :, DV:DA], 1.0)
            pool.memset(wgl[:, :, :].bitcast(F32), 0.0).then_inc(zero_ok, 1)
            chain = [0]

            def own(ins):
                chain[0] += 1
                ins.then_inc(p_own, 1)
                pool.wait_ge(p_own, chain[0])

            def rotate(t, src, done):
                if done:
                    pool.wait_ge(rope_ok, done)
                xx = src[:, t, :].rearrange("p (h a d) -> p h a d", h=H, a=2)
                cos = kc[:, K_COS + 64 * t:K_COS + 64 * (t + 1)].unsqueeze(1)
                sin = kc[:, K_SIN + 64 * t:K_SIN + 64 * (t + 1)].unsqueeze(1).to_broadcast([P, H, 64])
                a_ = rtmp[:, 0, :].rearrange("p (h a d) -> p h a d", h=H, a=2)
                b_ = rtmp[:, 1, :].rearrange("p (h a d) -> p h a d", h=H, a=2)
                nc.gpsimd.tensor_tensor(rtmp[:, 0, :].rearrange("p (g d) -> p g d", d=64), src[:, t, :].rearrange("p (g d) -> p g d", d=64),
                                cos.to_broadcast([P, 2 * H, 64]), ALU.mult)
                nc.gpsimd.tensor_tensor(b_[:, :, 0, :], xx[:, :, 1, :], sin, ALU.mult)
                own(nc.gpsimd.tensor_tensor(b_[:, :, 1, :], xx[:, :, 0, :], sin, ALU.mult))
                nc.gpsimd.tensor_tensor(xx[:, :, 0, :], a_[:, :, 0, :], b_[:, :, 0, :], ALU.subtract)
                last = nc.gpsimd.tensor_tensor(xx[:, :, 1, :], a_[:, :, 1, :], b_[:, :, 1, :], ALU.add)
                return last

            pool.wait_ge(c_in, 32)
            for t in range(TT):
                pool.wait_ge(free[t], B_RQ + 1)
                rotate(t, rqn, t).then_inc(rope_ok, 1)
            for t in range(TT):
                pool.wait_ge(free[t], B_RK + 1)
                own(rotate(t, rkn, TT + t))
                kk = rkn[:, t, :].rearrange("p (h d) -> p h d", h=H)
                nc.gpsimd.tensor_tensor(kk, kk, kc[:, K_KDEC:K_KDEC + H].unsqueeze(2).to_broadcast([P, H, DK]), ALU.mult).then_inc(rope_ok, 1)
            pool.wait_ge(lg_ps, 1)
            pool.memset(xg[:, :, :], 0.0).then_inc(zero_ok, 1)
            pool.wait_ge(h2_out, 16 * TT)
            pool.wait_ge(zero_ok, 4)

            def gather(E, e, par, reused=True):
                if reused:
                    pool.wait_ge(xT_ps, E - 1)
                pool.sem_inc(pool_past, 1)
                pool.tensor_copy(tok_now[:, par:par + 1], tok_tab[:, e:e + 1] if isinstance(e, int) else tok_tab[:, bass.ds(e, 1)]).then_inc(tok_c, 1)
                pool.wait_ge(tok_c, E + 1)
                pool.sem_inc(pool_past, 1)
                pool.indirect_dma_start(xg[:, par, :], None, h_dram, bass.IndirectOffsetOnAxis(ap=tok_now[:, par:par + 1], axis=0),
                                        bounds_check=T - 1, oob_is_err=False).then_inc(gat[par], 16)

            def scatter(E, e, par, first=False):
                if not first:
                    pool.wait_ge(sca, E * 16)
                    pool.sem_inc(out_ok, 1)
                pool.sem_inc(pool_past, 1)
                col = slice(e, e + 1) if isinstance(e, int) else bass.ds(e, 1)
                pool.tensor_copy(tok_out[:, :], tok_tab[:, col])
                pool.tensor_copy(w_now[:, par:par + 1], w_tab[:, col]).then_inc(w_c, 1)
                pool.wait_ge(yw_ok, E + 1)
                pool.wait_ge(w_c, E + 1)
                pool.sem_inc(pool_past, 1)
                pool.indirect_dma_start(x_dram, bass.IndirectOffsetOnAxis(ap=tok_out[:, :], axis=0), yo[:, par, :], None,
                                        bounds_check=T - 1, oob_is_err=False, compute_op=ALU.add).then_inc(sca, 16)

            def tail(r, i, t):
                src, s, loads = moe_raw(t)
                pool.wait_ge(wh_ok, r * R_PAIRS + i * 24 + (MIX_PAIRS + t + 1))
                nc.gpsimd.tensor_tensor(moe_split(wl, wl_more, t), src, moe_split(wh, wh_more, t).bitcast(F32), ALU.subtract).then_inc(pool_tail, 1)

            def moe_round(r):
                E0, first = r * NE, isinstance(r, int)

                def stage(i, e, par, first=False):
                    if not (isinstance(i, int) and e > NE - 4):
                        gather(E0 + i * 2 + (e + 3), i * 2 + (e + 3), 1 - par)
                    tail(r, i, E_PAIRS * e + POOL_PAIR)
                    scatter(E0 + i * 2 + (e - 1), i * 2 + (e - 1), 1 - par, first)

                pool.wait_ge(tab_ok, r + 1)
                for e in range(4):
                    gather(E0 + e, e, e % 2, e >= 2)
                tail(r, 0, POOL_PAIR)
                pool.wait_ge(wt_ok, r + 1)
                pool.wait_ge(st_in, 16 * TT)
                stage(0, 1, 1, first)
                stage(0, 2, 0)
                with pool.Fori(0, NE // 2 - 3, 1) as i:
                    stage(i, 3, 1)
                    stage(i, 4, 0)
                for e in range(NE - 3, NE):
                    stage(0, e, e % 2)
                scatter(E0 + NE - 1, NE - 1, 1)
                pool.wait_ge(sca, (E0 + NE) * 16)
                pool.sem_inc(r_done, 1)

            moe_round(0)
            pool.wait_ge(cnt_ok, 1)
            most = pool.value_load(cnt[0:1, 0:1], min_val=0, max_val=T)
            with pool.Fori(1, ROUNDS, 1) as r:
                with pool.If(most > r * CAP):
                    moe_round(r)
            pool.sem_inc(scat_ok, 1)


def constants():
    import numpy as np
    f = np.float32
    k = np.zeros((P, K_END), f)
    m, l = np.arange(P)[:, None], np.arange(P)[None, :]
    k[:, K_IDENT:K_IDENT + P] = m == l
    for h in range(H):
        g = GAMMA[h]
        k[:, K_RMASK + h * P:K_RMASK + (h + 1) * P] = (m <= l) * f(g ** -float(P))
        k[h, K_SELH + h * P:K_SELH + (h + 1) * P] = 1
        k[:, K_QDEC + h * P:K_QDEC + (h + 1) * P] = (g ** (l + 1.0)).astype(f)
        k[:, K_KDEC + h] = (g ** (P - 1.0 - m[:, 0]) * DK ** -0.5).astype(f)
    k[:, K_NOTYET:K_NOTYET + P] = np.where(m > l, f(BIG), f(0))
    k[:, K_BEFORE:K_BEFORE + P] = m < l
    k[:, K_SEL64:K_SEL64 + CAP] = (m % CAP) == l[:, :CAP]
    freq = (f(1.0) / (f(10000.0) ** (np.arange(0, DK, 2, dtype=f) / f(DK)))).astype(f)
    ang = np.arange(T, dtype=f)[:, None] * freq[None, :]
    for t in range(TT):
        k[:, K_COS + 64 * t:K_COS + 64 * (t + 1)] = np.cos(ang[t * P:(t + 1) * P])
        k[:, K_SIN + 64 * t:K_SIN + 64 * (t + 1)] = np.sin(ang[t * P:(t + 1) * P])
        k[:, K_TOK + t] = np.arange(P) + t * P - NO_TOKEN
    k[:, K_SLOT:K_SLOT + CAP] = np.arange(CAP)
    k[:, K_PRIO:K_PRIO + NE] = NE - np.arange(NE)
    return k


_INS = ['x', 'norm_mix_w', 'w_in', 'ret_gn_w', 'w_ret_branch', 'mlstm_conv_w', 'mlstm_conv_b', 'b_igate', 'b_fgate',
        'mlstm_gn_w', 'w_mlstm_branch', 'w_out', 'norm_ffn_w', 'w_group', 'b_group', 'w_expert_router',
        'b_expert_router', 'w_gate', 'w_up', 'w_down', 'norm_final_w']


def kernel(**inputs):
    import numpy as _np
    import concourse.bacc as _bacc
    from concourse import mybir as _mybir
    from concourse.bass_utils import run_bass_kernel_spmd as _run

    nc = _bacc.Bacc("TRN2", target_bir_lowering=False, num_devices=1)
    arrays, args = {}, []
    for name in _INS:
        a = _np.ascontiguousarray(inputs[name])
        arrays[f"in_{name}_dram"] = a
        args.append(nc.dram_tensor(f"in_{name}_dram", a.shape, _mybir.dt.from_np(a.dtype), kind="ExternalInput").ap())
    arrays["in_consts_dram"] = constants()
    args.append(nc.dram_tensor("in_consts_dram", arrays["in_consts_dram"].shape, F32, kind="ExternalInput").ap())
    args.append(nc.dram_tensor("out_0_dram", (1, T, D), F32, kind="ExternalOutput").ap())
    hybrid_block(nc, *args)
    r = _run(nc, [arrays], core_ids=[0])
    return r.results[0]["out_0_dram"]
```
